# Optimizing a Trainium2 kernel written in Bass

```python
import jax, jax.numpy as jnp
from jax import lax
import numpy as np

D_MODEL = 1024
BATCH = 1
SEQ = 256
DEPTH = 2

N_MIXERS = 3
Q_BLOCK = 128
ROPE_THETA = 500000.0
EPS = 1e-6
MAX_POS_OFFSET = 4096

SB_HEADS = 8
SB_HEAD_DIM = D_MODEL // SB_HEADS

MLA_HEADS = 8
MLA_Q_LORA = 256
MLA_KV_LORA = 128
MLA_NOPE_DIM = 128
MLA_ROPE_DIM = 64
MLA_V_DIM = D_MODEL // MLA_HEADS

DSA_HEADS = 8
DSA_KV_HEADS = 2
DSA_HEAD_DIM = 128
DSA_ROT_DIM = DSA_HEAD_DIM // 4
IDX_HEADS = 8
IDX_DIM = 64
IDX_ROT_DIM = IDX_DIM // 4
DSA_TOPK_MAX = 256
DSA_IN_WIDTH = (DSA_HEADS * DSA_HEAD_DIM + 2 * DSA_KV_HEADS * DSA_HEAD_DIM
                + IDX_HEADS * IDX_DIM + IDX_DIM + IDX_HEADS)

D_FF = 2816
N_EXPERTS = 8
TOP_K = 2
D_FF_EXPERT = 1408

kernel_name = 'hybrid_sb_mla_dsa_moe_adaln'

def _n_layers_of(period, phase):
    return len(range(phase, DEPTH, period))

def _rmsnorm(x, g):
    xf = x.astype(jnp.float32)
    y = xf * lax.rsqrt(jnp.mean(xf * xf, axis=-1, keepdims=True) + EPS)
    return (y * g.astype(jnp.float32)).astype(x.dtype)

def _rope_tables(positions, rot_dim):
    inv_freq = ROPE_THETA ** (-jnp.arange(0, rot_dim, 2, dtype=jnp.float32) / rot_dim)
    ang = positions.astype(jnp.float32)[..., None] * inv_freq
    return jnp.cos(ang), jnp.sin(ang)

def _apply_rope(x, cos, sin):
    rot = 2 * cos.shape[-1]
    if x.ndim == 4:
        cos, sin = cos[:, :, None, :], sin[:, :, None, :]
    xr = x[..., :rot].astype(jnp.float32)
    x1, x2 = xr[..., :rot // 2], xr[..., rot // 2:]
    xr = jnp.concatenate([x1 * cos - x2 * sin, x2 * cos + x1 * sin], axis=-1).astype(x.dtype)
    return jnp.concatenate([xr, x[..., rot:]], axis=-1)

def _swiglu(h, w_gu, w_down):
    a, b = jnp.split(h @ w_gu, 2, axis=-1)
    return (jax.nn.silu(a) * b) @ w_down

def _stick_breaking(h, w_in, w_out):
    B, S, _ = h.shape
    q, k, v = jnp.split((h @ w_in).reshape(B, S, 3 * SB_HEADS, SB_HEAD_DIM), 3, axis=2)
    scale = SB_HEAD_DIM ** -0.5
    outs = []
    for start in range(0, S, Q_BLOCK):
        end = start + Q_BLOCK
        z = jnp.einsum('bqhd,bkhd->bhqk', q[:, start:end], k[:, :end]).astype(jnp.float32) * scale
        mask = jnp.arange(end)[None, :] < jnp.arange(start, end)[:, None]
        log_beta = jax.nn.log_sigmoid(z)
        log_fail = jnp.where(mask, jax.nn.log_sigmoid(-z), 0.0)
        tail = lax.cumsum(log_fail, axis=3, reverse=True) - log_fail
        a = jnp.where(mask, jnp.exp(log_beta + tail), 0.0)
        outs.append(jnp.einsum('bhqk,bkhd->bqhd', a.astype(v.dtype), v[:, :end]))
    o = jnp.concatenate(outs, axis=1).reshape(B, S, SB_HEADS * SB_HEAD_DIM)
    return o @ w_out

def _causal_softmax_attention(q, k, v, scale):
    S = q.shape[1]
    outs = []
    for start in range(0, S, Q_BLOCK):
        end = start + Q_BLOCK
        s = jnp.einsum('bqhd,bkhd->bhqk', q[:, start:end], k[:, :end]).astype(jnp.float32) * scale
        mask = jnp.arange(end)[None, :] <= jnp.arange(start, end)[:, None]
        p = jax.nn.softmax(jnp.where(mask, s, -jnp.inf), axis=-1)
        outs.append(jnp.einsum('bhqk,bkhd->bqhd', p.astype(v.dtype), v[:, :end]))
    return jnp.concatenate(outs, axis=1)

def _mla(h, cos, sin, w_in, g_q, w_q_up, g_kv, w_kv_up, w_out):
    B, S, _ = h.shape
    c_q, c_kv, k_rope = jnp.split(h @ w_in, [MLA_Q_LORA, MLA_Q_LORA + MLA_KV_LORA], axis=-1)
    q = (_rmsnorm(c_q, g_q) @ w_q_up).reshape(B, S, MLA_HEADS, MLA_NOPE_DIM + MLA_ROPE_DIM)
    q_nope, q_rope = jnp.split(q, [MLA_NOPE_DIM], axis=-1)
    kv = (_rmsnorm(c_kv, g_kv) @ w_kv_up).reshape(B, S, MLA_HEADS, MLA_NOPE_DIM + MLA_V_DIM)
    k_nope, v = jnp.split(kv, [MLA_NOPE_DIM], axis=-1)
    q_rope = _apply_rope(q_rope, cos, sin)
    k_rope = _apply_rope(k_rope, cos, sin)
    q = jnp.concatenate([q_nope, q_rope], axis=-1)
    k = jnp.concatenate([k_nope, jnp.broadcast_to(k_rope[:, :, None, :], (B, S, MLA_HEADS, MLA_ROPE_DIM))], axis=-1)
    o = _causal_softmax_attention(q, k, v, (MLA_NOPE_DIM + MLA_ROPE_DIM) ** -0.5)
    return o.reshape(B, S, MLA_HEADS * MLA_V_DIM) @ w_out

def _dsa(h, cos_a, sin_a, cos_i, sin_i, w_in, g_kidx, w_out):
    B, S, _ = h.shape
    widths = [DSA_HEADS * DSA_HEAD_DIM, DSA_KV_HEADS * DSA_HEAD_DIM, DSA_KV_HEADS * DSA_HEAD_DIM,
              IDX_HEADS * IDX_DIM, IDX_DIM]
    cuts = [int(i) for i in np.cumsum(widths)]
    q, k, v, q_idx, k_idx, w_idx = jnp.split(h @ w_in, cuts, axis=-1)
    q = _apply_rope(q.reshape(B, S, DSA_HEADS, DSA_HEAD_DIM), cos_a, sin_a)
    k = _apply_rope(k.reshape(B, S, DSA_KV_HEADS, DSA_HEAD_DIM), cos_a, sin_a)
    v = v.reshape(B, S, DSA_KV_HEADS, DSA_HEAD_DIM)
    q_idx = _apply_rope(q_idx.reshape(B, S, IDX_HEADS, IDX_DIM), cos_i, sin_i)
    k_idx = _apply_rope(_rmsnorm(k_idx, g_kidx), cos_i, sin_i)
    w_idx = w_idx.astype(jnp.float32) * (IDX_HEADS ** -0.5)
    n_sel = min(DSA_TOPK_MAX, S // 4)
    group = DSA_HEADS // DSA_KV_HEADS
    gather = jax.vmap(lambda t, i: t[i])
    outs = []
    for start in range(0, S, Q_BLOCK):
        end = start + Q_BLOCK
        n_keys = min(S, max(end, n_sel))
        q_pos = jnp.arange(start, end)
        logits = jnp.einsum('bqhd,bkd->bqhk', q_idx[:, start:end], k_idx[:, :n_keys]).astype(jnp.float32) * IDX_DIM ** -0.5
        score = jnp.einsum('bqhk,bqh->bqk', jax.nn.relu(logits), w_idx[:, start:end])
        score = jnp.where(jnp.arange(n_keys)[None, None, :] <= q_pos[None, :, None], score, -jnp.inf)
        _, sel = lax.top_k(score, n_sel)
        valid = sel <= q_pos[None, :, None]
        k_sel = gather(k, sel)
        v_sel = gather(v, sel)
        qg = q[:, start:end].reshape(B, Q_BLOCK, DSA_KV_HEADS, group, DSA_HEAD_DIM)
        s = jnp.einsum('bqgnd,bqkgd->bqgnk', qg, k_sel).astype(jnp.float32) * DSA_HEAD_DIM ** -0.5
        p = jax.nn.softmax(jnp.where(valid[:, :, None, None, :], s, -jnp.inf), axis=-1)
        o = jnp.einsum('bqgnk,bqkgd->bqgnd', p.astype(v.dtype), v_sel)
        outs.append(o.reshape(B, Q_BLOCK, DSA_HEADS * DSA_HEAD_DIM))
    return jnp.concatenate(outs, axis=1) @ w_out

def _moe(h, w_router, b_router, w_gu, w_down):
    logits = (h @ w_router).astype(jnp.float32) + b_router.astype(jnp.float32)
    top_vals, top_idx = lax.top_k(logits, TOP_K)
    top_w = jax.nn.softmax(top_vals, axis=-1)
    gates = jnp.sum(jax.nn.one_hot(top_idx, N_EXPERTS, dtype=jnp.float32) * top_w[..., None], axis=-2)
    out = jnp.zeros_like(h)
    for e in range(N_EXPERTS):
        out = out + gates[..., e:e + 1].astype(h.dtype) * _swiglu(h, w_gu[e], w_down[e])
    return out

def setup_inputs(seed: int = 0) -> dict:
    key = jax.random.key(seed)
    keys = iter(jax.random.split(key, 40))

    def nrm(shape, scale):
        return jax.random.normal(next(keys), shape, jnp.float32) * scale

    def gain(shape):
        return 1.0 + nrm(shape, 0.02)

    d = D_MODEL
    n_a, n_b, n_c = _n_layers_of(N_MIXERS, 0), _n_layers_of(N_MIXERS, 1), _n_layers_of(N_MIXERS, 2)
    n_dense, n_moe = _n_layers_of(2, 0), _n_layers_of(2, 1)
    x = nrm((BATCH, SEQ, d), 1.0)
    c = nrm((BATCH, d), 1.0)
    offset = jax.random.randint(next(keys), (BATCH, 1), 0, MAX_POS_OFFSET, dtype=jnp.int32)
    positions = offset + jnp.arange(SEQ, dtype=jnp.int32)[None, :]
    return {
        'x': x,
        'c': c,
        'positions': positions,
        'ada_w': nrm((DEPTH, d, 6 * d), 0.5 * d ** -0.5),
        'ada_b': nrm((DEPTH, 6 * d), 0.02),
        'norm_g': gain((DEPTH, 4, d)),
        'sb_w_in': nrm((n_a, d, 3 * SB_HEADS * SB_HEAD_DIM), d ** -0.5),
        'sb_w_out': nrm((n_a, SB_HEADS * SB_HEAD_DIM, d), (SB_HEADS * SB_HEAD_DIM) ** -0.5),
        'mla_w_in': nrm((n_b, d, MLA_Q_LORA + MLA_KV_LORA + MLA_ROPE_DIM), d ** -0.5),
        'mla_g_q': gain((n_b, MLA_Q_LORA)),
        'mla_w_q_up': nrm((n_b, MLA_Q_LORA, MLA_HEADS * (MLA_NOPE_DIM + MLA_ROPE_DIM)), MLA_Q_LORA ** -0.5),
        'mla_g_kv': gain((n_b, MLA_KV_LORA)),
        'mla_w_kv_up': nrm((n_b, MLA_KV_LORA, MLA_HEADS * (MLA_NOPE_DIM + MLA_V_DIM)), MLA_KV_LORA ** -0.5),
        'mla_w_out': nrm((n_b, MLA_HEADS * MLA_V_DIM, d), (MLA_HEADS * MLA_V_DIM) ** -0.5),
        'dsa_w_in': nrm((n_c, d, DSA_IN_WIDTH), d ** -0.5),
        'dsa_g_kidx': gain((n_c, IDX_DIM)),
        'dsa_w_out': nrm((n_c, DSA_HEADS * DSA_HEAD_DIM, d), (DSA_HEADS * DSA_HEAD_DIM) ** -0.5),
        'ffn_w_gu': nrm((n_dense, d, 2 * D_FF), d ** -0.5),
        'ffn_w_down': nrm((n_dense, D_FF, d), D_FF ** -0.5),
        'moe_w_router': nrm((n_moe, d, N_EXPERTS), d ** -0.5),
        'moe_b_router': nrm((n_moe, N_EXPERTS), 0.01),
        'moe_w_gu': nrm((n_moe, N_EXPERTS, d, 2 * D_FF_EXPERT), d ** -0.5),
        'moe_w_down': nrm((n_moe, N_EXPERTS, D_FF_EXPERT, d), D_FF_EXPERT ** -0.5),
    }

def reference(x, c, positions, ada_w, ada_b, norm_g, sb_w_in, sb_w_out, mla_w_in, mla_g_q,
              mla_w_q_up, mla_g_kv, mla_w_kv_up, mla_w_out, dsa_w_in, dsa_g_kidx, dsa_w_out,
              ffn_w_gu, ffn_w_down, moe_w_router, moe_b_router, moe_w_gu, moe_w_down):
    cond = jax.nn.silu(c)
    cos_m, sin_m = _rope_tables(positions, MLA_ROPE_DIM)
    cos_a, sin_a = _rope_tables(positions, DSA_ROT_DIM)
    cos_i, sin_i = _rope_tables(positions, IDX_ROT_DIM)
    counters = [0, 0, 0]
    for layer in range(DEPTH):
        mod = (cond @ ada_w[layer] + ada_b[layer])[:, None, :]
        sh_m, sc_m, g_m, sh_f, sc_f, g_f = jnp.split(mod, 6, axis=-1)
        gn = norm_g[layer]
        h = _rmsnorm(x, gn[0]) * (1.0 + sc_m) + sh_m
        kind = layer % N_MIXERS
        j = counters[kind]
        counters[kind] += 1
        if kind == 0:
            y = _stick_breaking(h, sb_w_in[j], sb_w_out[j])
        elif kind == 1:
            y = _mla(h, cos_m, sin_m, mla_w_in[j], mla_g_q[j], mla_w_q_up[j], mla_g_kv[j],
                     mla_w_kv_up[j], mla_w_out[j])
        else:
            y = _dsa(h, cos_a, sin_a, cos_i, sin_i, dsa_w_in[j], dsa_g_kidx[j], dsa_w_out[j])
        x = x + g_m * _rmsnorm(y, gn[1])
        h = _rmsnorm(x, gn[2]) * (1.0 + sc_f) + sh_f
        f = layer // 2
        if layer % 2 == 0:
            y = _swiglu(h, ffn_w_gu[f], ffn_w_down[f])
        else:
            y = _moe(h, moe_w_router[f], moe_b_router[f], moe_w_gu[f], moe_w_down[f])
        x = x + g_f * _rmsnorm(y, gn[3])
    return x


_drawn_inputs = setup_inputs


def setup_inputs(seed=0):
    import zlib

    import numpy as np

    out = dict(_drawn_inputs(seed))
    spreads = {}
    factors = {'mla_g_q': 5.632, 'mla_g_kv': 3.383, 'moe_b_router': 3.139}
    for name, (base, spread) in spreads.items():
        noise = np.random.default_rng([zlib.crc32(name.encode()), seed]).standard_normal(out[name].shape)
        drawn = base * np.exp(spread * noise) if base else spread * noise
        out[name] = __import__('jax').numpy.asarray(drawn.astype(out[name].dtype))
    for name, factor in factors.items():
        out[name] = (out[name] * factor).astype(out[name].dtype)
    return out
```

```python
from contextlib import ExitStack

import concourse.bass as bass
from concourse import mybir

F32 = mybir.dt.float32
F32R = mybir.dt.float32r
I32 = mybir.dt.int32
ALU = mybir.AluOpType
ACT = mybir.ActivationFunctionType
AX = mybir.AxisListType

P = 128
T = 256
TC = T // P
D = 1024
DC = D // P
EPS = 1e-6
SB_H = 8
FF = 2816
FG = FF // 256
FC = FF // P
MLA_H = 8
QL, KVL, NOPE, ROPE = 256, 128, 128, 64
HR = ROPE // 2
MLA_IN = QL + KVL + ROPE
QW = NOPE + ROPE
KVW = 2 * P
E = 8
EF = 1408
EFC = EF // P
EG = (EFC + 1) // 2
CAP = P
R = 6
PIECE = 2048
NEG = -1.0e30
MAGIC = 12582912.0
TWO_PI = 6.283185307179586
PI_A, PI_B = 6.28125, 0.0019350051879882812
PI_C = TWO_PI - PI_A - PI_B
PI_MAX = 3.1415925

COND_ROW = 20
NROWS = 21


def trunk(nc, x_d, c_d, pos_d, ada_w, ada_b, norm_g, sb_w_in, sb_w_out, mla_w_in, mla_g_q, mla_w_q_up,
          mla_g_kv, mla_w_kv_up, mla_w_out, ffn_w_gu, ffn_w_down, w_router, b_router, moe_w_gu,
          moe_w_down, inv_freq, out_d):
    stream = []
    weight_no = {}
    first = {}

    def rows_view(w, k0, k, c0, c):
        return w.rearrange("(k p) n -> p k n", p=P)[:, k0:k0 + k, c0:c0 + c]

    def gate_up_view(w, k0, k, c0, c):
        return w.rearrange("(k p) (s n) -> p k s n", p=P, s=2)[:, k0:k0 + k, :, c0:c0 + c]

    def add_ada(layer, third, k):
        stream.append(("ada", (layer, third, k), ada_w[layer][k * P:(k + 1) * P, third * 2048:third * 2048 + 2048],
                       (2048,)))

    def add_weight(name, src, shape):
        first.setdefault(name, len(weight_no))
        weight_no[len(stream)] = len(weight_no)
        stream.append(("weight", name, src, shape))

    for k in range(DC):
        add_ada(0, 0, k)
    ada0 = [(t, k) for t in (1, 2) for k in range(DC)]
    for g in range(6):
        for h in range(2):
            add_weight("qkv", rows_view(sb_w_in[0], 4 * h, 4, g * 512, 512), (4, 512))
            add_ada(0, *ada0.pop(0))
    for t, k in ada0:
        add_ada(0, t, k)
    for g in range(2):
        for h in range(2):
            add_weight("sb_out", rows_view(sb_w_out[0], 4 * h, 4, g * 512, 512), (4, 512))
    ada1 = [(t, k) for t in range(3) for k in range(DC)]
    for j in range(FG):
        add_weight("gu", gate_up_view(ffn_w_gu[0], 0, 4, j * 256, 256), (4, 2, 256))
        add_weight("gu", gate_up_view(ffn_w_gu[0], 4, 4, j * 256, 256), (4, 2, 256))
        for _ in range(2 if j < 2 else 1):
            add_ada(1, *ada1.pop(0))
    for d in range(FG):
        add_weight("down", rows_view(ffn_w_down[0], 2 * d, 2, 0, D), (2, D))
        add_ada(1, *ada1.pop(0))
    assert not ada1
    for h in range(2):
        add_weight("mla_in", rows_view(mla_w_in[0], 4 * h, 4, 0, MLA_IN), (4, MLA_IN))
    for u in range(2):
        add_weight("q_up", rows_view(mla_w_q_up[0], 0, 2, u * 768, 768), (2, 768))
    add_weight("kv_up", rows_view(mla_w_kv_up[0], 0, 1, 0, 2048), (1, 2048))
    for g in range(2):
        for h in range(2):
            add_weight("mla_out", rows_view(mla_w_out[0], 4 * h, 4, g * 512, 512), (4, 512))
    N0, M0 = len(stream), len(weight_no)
    no_of = {m: n for n, m in weight_no.items()}
    ada_no = {p[1]: n for n, p in enumerate(stream) if p[0] == "ada"}
    NK = 3 * EG
    assert NK % R == 0 and NK % 3 == 0
    gw = [min(2, EFC - 2 * j) * P for j in range(EG)]
    dk = [min(2, EFC - 2 * d) for d in range(EG)]

    def expert_piece(e, k):
        if k < 2 * EG:
            j, h = divmod(k, 2)
            w = moe_w_gu[0, e].rearrange("(k p) (s n) -> p k s n", p=P, s=2)
            return w[:, 4 * h:4 * h + 4, :, j * 256:j * 256 + gw[j]], (4, 2, gw[j])
        d = k - 2 * EG
        w = moe_w_down[0, e].rearrange("(k p) n -> p k n", p=P)
        return w[:, 2 * d:2 * d + dk[d], :], (dk[d], D)

    def piece_elems(shape):
        n = 1
        for s in shape:
            n *= s
        return n

    ctx = ExitStack()
    with ctx:
        cursor = [(nc.sbuf_base + 63) // 32 * 32]

        def sb(name, shape, dt=F32, at=None):
            if at is None:
                at = cursor[0]
                cursor[0] += (4 * piece_elems(shape[1:]) + 31) // 32 * 32
            return nc.alloc_sbuf_tensor_at(name, shape, dt, offset=at)

        ring = [sb(f"ring{r}", [P, PIECE]) for r in range(R)]
        w_hi = [sb(f"w_hi{b}", [P, PIECE], F32R) for b in range(2)]
        w_lo = [sb(f"w_lo{b}", [P, PIECE], F32R) for b in range(2)]
        x = sb("x", [P, TC, D])
        xhat_at = cursor[0]
        xhat = sb("xhat", [P, TC, D])
        hT_at = cursor[0]
        hT_hi = sb("hT_hi", [P, DC, T], F32R)
        hT_lo = sb("hT_lo", [P, DC, T], F32R)
        gate = [sb(f"gate{w}", [P, D]) for w in range(2)]
        rows = sb("rows", [NROWS, D])
        ident = sb("ident", [P, P])
        ident_r = sb("ident_r", [P, P], F32R)
        ones = sb("ones", [P, P])
        neg_ge = sb("neg_ge", [P, P])
        neg_one = sb("neg_one", [P, P])
        before = sb("before", [P, P])
        causal = sb("causal", [P, P])
        slot_no = sb("slot_no", [P, P])
        cols = sb("cols", [P, DC, NROWS])
        lat_rows = sb("lat_rows", [3, P])
        lat_g = sb("lat_g", [P, 3])
        cond = sb("cond", [P, DC])
        shift = sb("shift", [P, 4, DC])
        scale = sb("scale", [P, 4, DC])
        ssq = sb("ssq", [P, 10, TC])
        rstd = sb("rstd", [P, 10, TC])
        freq = sb("freq", [1, HR])
        pos_i = sb("pos_i", [P, TC], I32)
        pos_f = sb("pos_f", [P, TC])
        ang = sb("ang", [P, 2, TC, HR])
        turns = sb("turns", [P, 2, TC, HR])
        trig = sb("trig", [P, 2, TC, HR])
        wr = sb("wr", [P, DC, E])
        br = sb("br", [1, E])
        lg = sb("lg", [P, TC, E])
        top8 = sb("top8", [P, TC, 8])
        eq = sb("eq", [P, TC, E])
        eight = sb("eight", [P, E])
        kmax = sb("kmax", [P, TC, 8])
        one1 = sb("one1", [P, TC, E])
        one2 = sb("one2", [P, TC, E])
        lg2 = sb("lg2", [P, TC, E])
        top8b = sb("top8b", [P, TC, 8])
        diff = sb("diff", [P, TC])
        wt = sb("wt", [P, 2, TC])
        member = sb("member", [P, TC, E])
        NV = 2 * E + 1
        visit = sb("visit", [P, NV, 3 * TC])
        cur = sb("cur", [P, 3 * TC])
        count_f = sb("count_f", [P, 1])
        n_end = sb("n_end", [P, 1], I32)
        acc_at = cursor[0]
        acc = sb("acc", [P, 6 * D])
        base = cursor[0]

        t32 = sb("t32", [P, DC, T], at=base + 36864)
        junk = sb("junk", [P, D], at=base)
        qkv = sb("qkv", [P, TC, 3 * D], at=base)
        qkT = sb("qkT", [P, SB_H, 2 * T], at=base + 24576)
        stick = [sb(f"stick{g}", [P, 4, 3, P], at=base + 12288 * g) for g in range(2)]
        gT_hi = sb("gT_hi", [P, FC, T], F32R, at=base)
        gT_lo = sb("gT_lo", [P, FC, T], F32R, at=base + 22528)
        hid = [sb(f"hid{b}", [P, TC, 256], at=xhat_at + 2048 * b) for b in range(2)]
        qn = sb("qn", [P, TC, MLA_H * QW], at=base)
        kvn = sb("kvn", [P, TC, MLA_H * KVW], at=base + 12288)
        lat = sb("lat", [P, TC, QL + KVL], at=base + 28672)
        kr = sb("kr", [P, TC, ROPE], at=base + 31744)
        cT = sb("cT", [P, 3, T], at=base + 32256)
        cT_hi = sb("cT_hi", [P, 3, T], F32R, at=base + 35328)
        cT_lo = sb("cT_lo", [P, 3, T], F32R, at=base + 38400)
        krT = sb("krT", [ROPE, T], at=base + 41472)
        rt = sb("rt", [P, 4, MLA_H, HR], at=xhat_at)
        prob0 = sb("prob0", [P, 4, 3, P], at=base + 35328)
        prob1 = sb("prob1", [P, 4, 3, P], at=base + 28672)
        prob = [prob0, prob1]
        qnT = sb("qnT", [P, MLA_H, T], at=acc_at)
        knT = sb("knT", [P, MLA_H, T], at=acc_at + 8192)
        qrT = sb("qrT", [ROPE, MLA_H, T], at=acc_at + 16384)
        nmax = sb("nmax", [P, 2, TC, 4], at=base + 42496)
        psum_p = sb("psum_p", [P, 2, TC, 4], at=base + 42560)
        rsum = sb("rsum", [P, 2, TC, 4], at=base + 42624)
        macc = sb("macc", [P, TC, D], at=base)
        xe32 = sb("xe32", [P, DC, P], at=base + 8192)
        xe_hi = sb("xe_hi", [P, DC, P], F32R, at=base + 12288)
        xe_lo = sb("xe_lo", [P, DC, P], F32R, at=base + 16384)
        eT_hi = sb("eT_hi", [P, EFC, P], F32R, at=base + 20480)
        eT_lo = sb("eT_lo", [P, EFC, P], F32R, at=base + 26112)
        esil = [sb(f"esil{b}", [P, 256], at=base + 31744 + 1024 * b) for b in range(2)]
        ehid = [sb(f"ehid{b}", [P, 256], at=base + 33792 + 1024 * b) for b in range(2)]
        ye_hi = sb("ye_hi", [P, D], F32R, at=base + 35840)
        ye_lo = sb("ye_lo", [P, D], F32R, at=base + 39936)
        pick = sb("pick", [P, TC, P], F32R, at=acc_at)
        spread = sb("spread", [P, T], F32R, at=acc_at + 1024)
        mjunk = sb("mjunk", [P, D], at=acc_at + 4096)
        NB = 3
        m_hi = w_hi + [sb("m_hi2", [P, PIECE], F32R, at=acc_at + 8192)]
        m_lo = w_lo + [sb("m_lo2", [P, PIECE], F32R, at=acc_at + 16384)]
        xhat_hi = sb("xhat_hi", [P, TC, D], F32R, at=hT_at)
        xhat_lo = sb("xhat_lo", [P, TC, D], F32R, at=hT_at + 8192)
        assert base + 45056 <= nc.sbuf_usable_end, (base, nc.sbuf_usable_end)

        ps = ctx.enter_context(nc.psum_tensor("ps", [P, 8, 512], F32))

        def sem(name):
            return ctx.enter_context(nc.semaphore(name))

        landed = [sem(f"landed{r}") for r in range(R)]
        s_x, s_rows, s_small, s_out = sem("s_x"), sem("s_rows"), sem("s_small"), sem("s_out")
        freed = sem("freed")
        hi_done = sem("hi_done")
        used = sem("used")
        consts, idn = sem("consts"), sem("idn")
        rowsT = sem("rowsT")
        cols_ok = sem("cols_ok")
        cond_ok = sem("cond_ok")
        mod_mm, mod_ok = sem("mod_mm"), sem("mod_ok")
        gate_mm, gain_ok, gate_ok = sem("gate_mm"), sem("gain_ok"), sem("gate_ok")
        ss_done, var_done, root_done = sem("ss_done"), sem("var_done"), sem("root_done")
        rstd_done = sem("rstd_done")
        x_done = sem("x_done")
        xhat_done = sem("xhat_done")
        tr_done = sem("tr_done")
        t_done, hThi, hTlo = sem("t_done"), sem("hThi"), sem("hTlo")
        ev_qkv = sem("ev_qkv")
        qkT_mm, qkT_d, qkT_a = sem("qkT_mm"), sem("qkT_d"), sem("qkT_a")
        z_mm, ln_ok, sp_ok = sem("z_mm"), sem("ln_ok"), sem("sp_ok")
        sp_masked, tail_mm, a_ok, a_masked, pv_mm = (sem("sp_masked"), sem("tail_mm"), sem("a_ok"),
                                                     sem("a_masked"), sem("pv_mm"))
        oT_hi, oT_lo = sem("oT_hi"), sem("oT_lo")
        sil_ok, hid_ok, hid_T = sem("sil_ok"), sem("hid_ok"), sem("hid_T")
        gThi, gTlo = sem("gThi"), sem("gTlo")
        trig_a, trig_ok = sem("trig_a"), sem("trig_ok")
        lat_ok, lat_T, cT_ok, cThi, cTlo = sem("lat_ok"), sem("lat_T"), sem("cT_ok"), sem("cThi"), sem("cTlo")
        ev_q, ev_kv, rope_ok = sem("ev_q"), sem("ev_kv"), sem("rope_ok")
        qT_mm, qT_ok, kT_mm, kT_ok = sem("qT_mm"), sem("qT_ok"), sem("kT_mm"), sem("kT_ok")
        rT_mm, rT_a, rT_d = sem("rT_mm"), sem("rT_a"), sem("rT_d")
        s_mm, smax_ok, exp_ok, prob_ok, pT_mm, pT_ok = (sem("s_mm"), sem("smax_ok"), sem("exp_ok"),
                                                        sem("prob_ok"), sem("pT_mm"), sem("pT_ok"))
        lg_mm, wt_a, wt_ok, member_ok, pos_mm, visit_ok = (sem("lg_mm"), sem("wt_a"), sem("wt_ok"),
                                                           sem("member_ok"), sem("pos_mm"), sem("visit_ok"))
        dve_step, act_step = sem("dve_step"), sem("act_step")
        e_step = sem("e_step")
        e_pick, e_gath, e_t, e_xhi, e_xlo = sem("e_pick"), sem("e_gath"), sem("e_t"), sem("e_xhi"), sem("e_xlo")
        e_sil, e_hid, e_hidT, e_ghi, e_glo = (sem("e_sil"), sem("e_hid"), sem("e_hidT"), sem("e_ghi"),
                                              sem("e_glo"))
        e_y, e_ylo, e_sc, e_add, e_pT, e_blank = (sem("e_y"), sem("e_ylo"), sem("e_sc"), sem("e_add"),
                                                  sem("e_pT"), sem("e_blank"))
        xs_hi, xs_lo = sem("xs_hi"), sem("xs_lo")

        filled, total = [], [0] * R
        for n in range(N0 + NK):
            shape = stream[n][3] if n < N0 else expert_piece(0, n - N0)[1]
            total[n % R] += 16 * (2 if len(shape) == 3 else 1)
            filled.append(total[n % R])
        before_visits = [max([filled[n] for n in range(r, N0, R)]) for r in range(R)]
        per_visit = [total[r] - before_visits[r] for r in range(R)]

        def wait_piece(eng, n):
            eng.wait_ge(landed[n % R], filled[n])

        def wait_expert_piece(eng, i, k):
            n = N0 + k
            eng.wait_ge(landed[n % R], filled[n] + per_visit[n % R] * i)

        def slot(n, shape):
            return ring[n % R][:, 0:piece_elems(shape)]

        def load(eng, n, src, shape):
            dst = slot(n, shape)
            if len(shape) == 3:
                dst = dst.rearrange("p (k s n) -> p k s n", k=shape[0], s=shape[1])
                for s in range(2):
                    eng.dma_start(dst[:, :, s, :], src[:, :, s, :]).then_inc(landed[n % R], 16)
            elif len(shape) == 2:
                eng.dma_start(dst.rearrange("p (k n) -> p k n", k=shape[0]), src).then_inc(landed[n % R], 16)
            else:
                eng.dma_start(dst, src).then_inc(landed[n % R], 16)

        def chain(eng, step_sem):
            count = [0]

            def link(ins):
                ins.then_inc(step_sem, 1)
                count[0] += 1
                eng.wait_ge(step_sem, count[0])
            return link

        block = ctx.enter_context(nc.Block())

        @block.sync
        def _(sp):
            for n, (_, _, src, shape) in enumerate(stream):
                if n >= R:
                    sp.wait_ge(freed, n - R + 1)
                load(sp, n, src, shape)

            def visit_experts(lo, hi):
                with sp.Fori(lo, hi) as i:
                    for k in range(NK):
                        sp.wait_ge(freed, N0 + k - R + 1 + NK * i)
                        src, shape = expert_piece(i - lo, k)
                        load(sp, N0 + k, src, shape)

            visit_experts(0, E)
            sp.wait_ge(visit_ok, 1)
            last = sp.value_load(n_end[0:1, 0:1], min_val=E, max_val=2 * E)
            with sp.If(last > E):
                visit_experts(E, 2 * E)

        @block.gpsimd
        def _(pool):
            pool.memset(ones[:, :], 1.0).then_inc(consts, 1)
            pool.memset(neg_one[:, :], -1.0).then_inc(consts, 1)
            pool.memset(causal[:, :], 0.0).then_inc(consts, 1)
            pool.memset(ident[:, :], 0.0).then_inc(consts, 1)
            pool.iota(slot_no[:, :], pattern=[[1, P]], base=0, channel_multiplier=0,
                      allow_small_or_imprecise_dtypes=True).then_inc(consts, 1)
            pool.iota(eight[:, :], pattern=[[-1, E]], base=E, channel_multiplier=0,
                      allow_small_or_imprecise_dtypes=True).then_inc(consts, 1)
            pool.wait_ge(consts, 6)
            pool.affine_select(out=ident[:, :], in_=ident[:, :], compare_op=ALU.not_equal, fill=1.0, base=0,
                               pattern=[[-1, P]], channel_multiplier=1).then_inc(idn, 1)
            pool.affine_select(out=neg_ge[:, :], in_=neg_one[:, :], compare_op=ALU.is_ge, fill=0.0, base=0,
                               pattern=[[-1, P]], channel_multiplier=1).then_inc(consts, 1)
            pool.affine_select(out=before[:, :], in_=ones[:, :], compare_op=ALU.is_gt, fill=0.0, base=0,
                               pattern=[[1, P]], channel_multiplier=-1).then_inc(consts, 1)
            pool.affine_select(out=causal[:, :], in_=causal[:, :], compare_op=ALU.is_ge, fill=NEG, base=0,
                               pattern=[[-1, P]], channel_multiplier=1).then_inc(consts, 1)
            for ready, masked in ((sp_ok, sp_masked), (a_ok, a_masked)):
                for g in range(2):
                    pool.wait_ge(ready, g + 1)
                    for b in (0, 2):
                        pool.affine_select(out=stick[g][:, :, b, :], in_=stick[g][:, :, b, :], compare_op=ALU.is_gt,
                                           fill=0.0, base=0, pattern=[[0, 4], [1, P]], channel_multiplier=-1)\
                            .then_inc(masked, 1)

        @block.scalar
        def _(act):
            link = chain(act, act_step)
            for l in range(2):
                act.dma_start(rows[6 * l:6 * l + 6, :], ada_b[l].rearrange("(s n) -> s n", s=6)).then_inc(s_rows, 16)
                act.dma_start(rows[12 + 4 * l:16 + 4 * l, :], norm_g[l]).then_inc(s_rows, 16)
            act.dma_start(rows[COND_ROW:NROWS, :], c_d).then_inc(s_rows, 16)
            act.dma_start(x[:, :, :], x_d[0].rearrange("(c p) n -> p c n", p=P)).then_inc(s_x, 16)
            act.dma_start(lat_rows[0:2, :], mla_g_q[0].rearrange("(k n) -> k n", n=P)).then_inc(s_rows, 16)
            act.dma_start(lat_rows[2:3, :], mla_g_kv).then_inc(s_rows, 16)
            act.dma_start(freq[:, :], inv_freq).then_inc(s_rows, 16)
            act.dma_start(pos_i[:, :], pos_d[0].rearrange("(c p) -> p c", p=P),
                          allow_slow_non_contiguous=True).then_inc(s_small, 16)
            act.dma_start(wr[:, :, :], w_router[0].rearrange("(k p) n -> p k n", p=P)).then_inc(s_small, 16)
            act.dma_start(br[:, :], b_router).then_inc(s_small, 16)

            def hi(m):
                n = no_of[m]
                wait_piece(act, n)
                if m >= 2:
                    act.wait_ge(used, m - 1)
                cols_n = piece_elems(stream[n][3])
                act.activation(w_hi[m % 2][:, 0:cols_n], ring[n % R][:, 0:cols_n], ACT.Copy).then_inc(hi_done, 1)

            def squares(u, c, src, out=junk):
                if TC * u + c:
                    act.wait_ge(ss_done, TC * u + c)
                dst = out[:, 0:piece_elems(src.shape[1:])]
                if len(src.shape) == 3:
                    dst = dst.rearrange("p (a b) -> p a b", a=src.shape[1])
                act.activation(dst, src, ACT.Square, accum_out=ssq[:, u, c:c + 1]).then_inc(ss_done, 1)

            def root(u):
                act.wait_ge(var_done, u + 1)
                act.activation(rstd[:, u, :], ssq[:, u, :], ACT.Sqrt).then_inc(root_done, 1)

            def modulated_hi(v):
                for b in range(4):
                    act.wait_ge(t_done, 4 * v + b + 1)
                    act.activation(hT_hi[:, 2 * b:2 * b + 2, :], t32[:, 2 * b:2 * b + 2, :], ACT.Copy)\
                        .then_inc(hThi, 1)

            def gain(n, w):
                act.wait_ge(gate_mm, n + 1)
                act.activation(gate[w][:, :].rearrange("p (a b) -> p a b", a=2), ps[:, 6:8, :], ACT.Copy)\
                    .then_inc(gain_ok, 1)

            def head_hi(g, n):
                act.wait_ge(pv_mm, n + 1)
                act.activation(hT_hi[:, 4 * g:4 * g + 4, :], ps[:, 4 * g:4 * g + 4, 0:T], ACT.Copy).then_inc(oT_hi, 1)

            act.wait_ge(s_x, 16)
            for c in range(TC):
                squares(0, c, x[:, c, :])
            root(0)
            act.wait_ge(cols_ok, 1)
            act.activation(cond[:, :], cols[:, :, COND_ROW], ACT.Silu).then_inc(cond_ok, 1)
            act.wait_ge(trig_a, 1)
            act.activation(trig[:, :, :, :], ang[:, :, :, :], ACT.Sin).then_inc(trig_ok, 1)
            hi(0)
            hi(1)
            modulated_hi(0)
            for g in range(6):
                if g < 5:
                    hi(2 * g + 2)
                    hi(2 * g + 3)
                act.wait_ge(used, 2 * g + 2)
                for c in range(TC):
                    act.activation(qkv[:, c, g * 512:(g + 1) * 512], ps[:, 2 * (g % 4) + c, :], ACT.Copy,
                                   scale=(float(P) ** -0.5 if g < 2 else 1.0)).then_inc(ev_qkv, 1)
            for h in range(1, SB_H, 2):
                act.wait_ge(qkT_mm, h + 1)
                act.activation(qkT[:, h, :], ps[:, h, :], ACT.Copy).then_inc(qkT_a, 1)
            for g in range(2):
                act.wait_ge(z_mm, g + 1)
                link(act.activation(stick[g][:, :, :, :].rearrange("p h b n -> p h (b n)"),
                                    ps[:, 4 * g:4 * g + 4, 0:3 * P], ACT.Abs))
                link(act.activation(stick[g][:, :, :, :], stick[g][:, :, :, :], ACT.Exp, scale=-1.0))
                act.activation(stick[g][:, :, :, :], stick[g][:, :, :, :], ACT.Ln, bias=1.0).then_inc(ln_ok, 1)
            for g in range(2):
                act.wait_ge(tail_mm, g + 1)
                act.activation(stick[g][:, :, :, :], ps[:, 4 * g:4 * g + 4, 0:3 * P].rearrange(
                    "p h (b n) -> p h b n", b=3), ACT.Exp).then_inc(a_ok, 1)
            M = first["sb_out"]
            hi(M)
            hi(M + 1)
            for g in range(2):
                head_hi(g, g)
            gain(0, 0)
            for k in range(2, 4):
                hi(M + k)
            act.wait_ge(used, M + 4)
            for c in range(TC):
                squares(1, c, ps[:, 2 * c:2 * c + 2, :])
            root(1)
            for c in range(TC):
                act.wait_ge(x_done, c + 1)
                squares(2, c, x[:, c, :])
            root(2)
            hi(M + 4)
            hi(M + 5)
            modulated_hi(1)
            gain(1, 1)
            M = first["gu"]

            def g_hi(j):
                act.wait_ge(hid_T, j + 1)
                act.activation(gT_hi[:, 2 * j:2 * j + 2, :], ps[:, 4 + j % 2, :].rearrange("p (a b) -> p a b", a=2),
                               ACT.Copy).then_inc(gThi, 1)

            for j in range(FG):
                hi(M + 2 * j + 2)
                if j >= 1:
                    g_hi(j - 1)
                hi(M + 2 * j + 3)
                act.wait_ge(used, M + 2 * j + 2)
                if j >= 2:
                    act.wait_ge(hid_T, j - 1)
                act.activation(hid[j % 2][:, :, :], ps[:, 2 * (j % 2):2 * (j % 2) + 2, 0:256], ACT.Silu)\
                    .then_inc(sil_ok, 1)
            M = first["down"]
            hi(M + 2)
            g_hi(FG - 1)
            for d in range(3, FG):
                hi(M + d)
            act.wait_ge(used, M + FG)
            for c in range(TC):
                squares(3, c, ps[:, 2 * c:2 * c + 2, :])
            root(3)
            for c in range(TC):
                act.wait_ge(x_done, TC + c + 1)
                squares(4, c, x[:, c, :])
            root(4)
            M = first["mla_in"]
            hi(M)
            hi(M + 1)
            modulated_hi(2)
            gain(2, 0)
            gain(3, 1)
            hi(M + 2)
            hi(M + 3)
            act.wait_ge(used, M + 2)
            for c in range(TC):
                squares(5, c, ps[:, c, 0:QL])
            for c in range(TC):
                squares(6, c, ps[:, c, QL:QL + KVL])
            root(5)
            root(6)
            act.wait_ge(cT_ok, 1)
            act.activation(cT_hi[:, :, :], cT[:, :, :], ACT.Copy).then_inc(cThi, 1)
            hi(M + 4)
            for u in range(2):
                act.wait_ge(used, M + 3 + u)
                for c in range(TC):
                    for s in range(2):
                        act.activation(qn[:, c, u * 768 + s * 384:u * 768 + (s + 1) * 384],
                                       ps[:, 4 * (1 - u) + 2 * c + s, 0:384], ACT.Copy,
                                       scale=float(QW) ** -0.5).then_inc(ev_q, 1)
            act.wait_ge(used, M + 5)
            for c in (1, 0):
                for s in range(4):
                    act.activation(kvn[:, c, s * 512:(s + 1) * 512], ps[:, 4 * c + s, :], ACT.Copy).then_inc(ev_kv, 1)
            act.wait_ge(qT_mm, 1)
            act.activation(qnT[:, :, :].rearrange("p (b a) t -> p b (a t)", b=4), ps[:, 4:8, :], ACT.Copy)\
                .then_inc(qT_ok, 1)
            act.wait_ge(rT_mm, 1)
            act.activation(qrT[:, :, :].rearrange("p (b a) t -> p b (a t)", b=4), ps[0:ROPE, 4:8, :], ACT.Copy)\
                .then_inc(rT_a, 1)
            for g in range(2):
                act.wait_ge(smax_ok, g + 1)
                for h in range(4):
                    act.activation(prob[g][:, h, 0, :], prob[g][:, h, 0, :], ACT.Exp, bias=nmax[:, g, 0, h:h + 1],
                                   accum_out=psum_p[:, g, 0, h:h + 1]).then_inc(exp_ok, 1)
                    act.activation(prob[g][:, h, 1:3, :], prob[g][:, h, 1:3, :], ACT.Exp, bias=nmax[:, g, 1, h:h + 1],
                                   accum_out=psum_p[:, g, 1, h:h + 1]).then_inc(exp_ok, 1)
            for g in range(2):
                head_hi(g, 2 + g)
            M = first["mla_out"]
            for k in range(4):
                hi(M + k)
            act.wait_ge(used, M + 4)
            for c in range(TC):
                squares(7, c, ps[:, 2 * c:2 * c + 2, :], mjunk)
            root(7)
            for c in range(TC):
                act.wait_ge(x_done, 2 * TC + c + 1)
                squares(8, c, x[:, c, :], mjunk)
            root(8)
            modulated_hi(3)
            act.wait_ge(wt_a, 1)
            act.activation(wt[:, 1, :], diff[:, :], ACT.Exp).then_inc(wt_ok, 1)

            act.wait_ge(lg_mm, 1)
            act.activation(xhat_hi[:, :, :], xhat[:, :, :], ACT.Copy).then_inc(xs_hi, 1)

            def x_out(n):
                for b in range(2):
                    act.wait_ge(e_gath, n + b + 1)
                    for a in range(4):
                        k = 4 * b + a
                        ins = act.activation(xe32[:, k, :], ps[:, b, a * P:(a + 1) * P], ACT.Identity,
                                             scale=scale[:, 3, k:k + 1], bias=shift[:, 3, k:k + 1])
                    ins.then_inc(e_t, 1)
                for b in range(2):
                    act.wait_ge(e_t, n + b + 1)
                    act.activation(xe_hi[:, 4 * b:4 * b + 4, :], xe32[:, 4 * b:4 * b + 4, :], ACT.Copy)\
                        .then_inc(e_xhi, 1)

            def y_out(n):
                act.wait_ge(used, n)
                act.activation(ye_hi[:, :].rearrange("p (a b) -> p a b", a=2), ps[:, 4:6, :], ACT.Copy)\
                    .then_inc(e_y, 1)

            x_out(0)
            act.wait_ge(visit_ok, 1)
            last = act.value_load(n_end[0:1, 0:1], min_val=E, max_val=2 * E)
            act.wait_ge(e_blank, 1)
            with act.Fori(0, last) as i:
                def ehi(k):
                    wait_expert_piece(act, i, k)
                    act.wait_ge(used, M0 + k - NB + 1 + NK * i)
                    n_c = piece_elems(expert_piece(0, k)[1])
                    act.activation(m_hi[k % NB][:, 0:n_c], ring[(N0 + k) % R][:, 0:n_c], ACT.Copy)\
                        .then_inc(hi_done, 1)

                def eg_hi(j):
                    act.wait_ge(e_hidT, EG * i + j + 1)
                    n_f = gw[j] // P
                    act.activation(eT_hi[:, 2 * j:2 * j + n_f, :].rearrange("p a b -> p (a b)"),
                                   ps[:, 2 + j % 2, 0:gw[j]], ACT.Copy).then_inc(e_ghi, 1)

                ehi(0)
                ehi(1)
                ehi(2)
                y_out(M0 + NK * i)
                for j in range(EG):
                    ehi(2 * j + 3)
                    if j >= 1:
                        eg_hi(j - 1)
                    act.wait_ge(used, M0 + 2 * j + 2 + NK * i)
                    if j >= 2:
                        act.wait_ge(e_hid, EG * i + j - 1)
                    act.activation(esil[j % 2][:, 0:gw[j]], ps[:, j % 2, 0:gw[j]], ACT.Silu).then_inc(e_sil, 1)
                    if j == 4:
                        act.wait_ge(e_pT, i + 1)
                        act.activation(spread[:, :], ps[:, 6, 0:T], ACT.Copy)
                    ehi(2 * j + 4)
                ehi(2 * EG + 3)
                eg_hi(EG - 1)
                ehi(2 * EG + 4)
                x_out(2 * i + 2)
                ehi(2 * EG + 5)
            y_out(M0 + NK * last)
            act.wait_ge(e_add, 2 * last + 2)
            for c in range(TC):
                squares(9, c, macc[:, c, :], mjunk)
            root(9)
            for c in range(TC):
                act.wait_ge(x_done, 3 * TC + c + 1)
                act.dma_start(out_d[0, c * P:(c + 1) * P, :], x[:, c, :]).then_inc(s_out, 16)
            act.wait_ge(s_out, 32)

        @block.vector
        def _(dve):
            link = chain(dve, dve_step)
            pieces = [0]

            def lo(m):
                n = no_of[m]
                assert n == pieces[0], (n, pieces)
                pieces[0] += 1
                dve.wait_ge(hi_done, m + 1)
                cols_n = piece_elems(stream[n][3])
                dve.tensor_tensor(w_lo[m % 2][:, 0:cols_n], ring[n % R][:, 0:cols_n],
                                  w_hi[m % 2][:, 0:cols_n].bitcast(F32), ALU.subtract).then_inc(freed, 1)

            def ada(count):
                for _ in range(count):
                    n = pieces[0]
                    assert stream[n][0] == "ada"
                    pieces[0] += 1
                    _, third, k = stream[n][1]
                    dst = acc[:, third * 2048:third * 2048 + 2048]
                    wait_piece(dve, n)
                    if k == 0:
                        dve.tensor_scalar(dst, ring[n % R][:, :], cond[:, 0:1], None, ALU.mult).then_inc(freed, 1)
                    else:
                        dve.wait_ge(freed, n)
                        dve.scalar_tensor_tensor(dst, ring[n % R][:, :], cond[:, k:k + 1], dst, ALU.mult,
                                                 ALU.add).then_inc(freed, 1)

            def rms(u, width):
                dve.wait_ge(ss_done, TC * (u + 1))
                dve.tensor_scalar(ssq[:, u, :], ssq[:, u, :], 1.0 / width, EPS, ALU.mult, ALU.add).then_inc(var_done, 1)
                dve.wait_ge(root_done, u + 1)
                dve.reciprocal(rstd[:, u, :], rstd[:, u, :]).then_inc(rstd_done, 1)
                dve.wait_ge(rstd_done, u + 1)

            def normalise(u):
                for c in range(TC):
                    dve.tensor_scalar(xhat[:, c, :], x[:, c, :], rstd[:, u, c:c + 1], None, ALU.mult)\
                        .then_inc(xhat_done, 1)

            def modulated(v, between=()):
                def cut(b):
                    dve.wait_ge(hThi, 4 * v + b + 1)
                    dve.tensor_tensor(hT_lo[:, 2 * b:2 * b + 2, :], t32[:, 2 * b:2 * b + 2, :],
                                      hT_hi[:, 2 * b:2 * b + 2, :].bitcast(F32), ALU.subtract).then_inc(hTlo, 1)

                for b in range(4):
                    dve.wait_ge(tr_done, 4 * v + b + 1)
                    for a in range(2):
                        k = 2 * b + a
                        ins = dve.tensor_scalar(t32[:, k, :], ps[:, b, a * T:(a + 1) * T], scale[:, v, k:k + 1],
                                                shift[:, v, k:k + 1], ALU.mult, ALU.add)
                    ins.then_inc(t_done, 1)
                    if b:
                        cut(b - 1)
                cut(3)

            def mod_cols(v):
                l, w = divmod(v, 2)
                dve.wait_ge(mod_mm, v + 1)
                dve.tensor_tensor(shift[:, v, :], ps[:, 4, 0:DC], cols[:, :, 6 * l + 3 * w], ALU.add)
                link(dve.tensor_tensor(scale[:, v, :], ps[:, 4, DC:2 * DC], cols[:, :, 6 * l + 3 * w + 1], ALU.add))
                dve.scalar_tensor_tensor(scale[:, v, :], scale[:, v, :], 1.0, cols[:, :, 12 + 4 * l + 2 * w],
                                         ALU.add, ALU.mult).then_inc(mod_ok, 1)
                dve.wait_ge(mod_ok, v + 1)

            def gate_rows(n, w):
                dve.wait_ge(gain_ok, n + 1)
                dve.wait_ge(gate_mm, n + 1)
                g = gate[w][:, :].rearrange("p (a b) -> p a b", a=2)
                dve.tensor_tensor(g, ps[:, 4:6, :], g, ALU.mult).then_inc(gate_ok, 1)

            def residual(q, u, srcs, w):
                rms(u, D)
                for c in range(TC):
                    dst, g = xhat[:, c, :], gate[w][:, :]
                    if len(srcs[c].shape) == 3:
                        dst, g = (a.rearrange("p (a b) -> p a b", a=2) for a in (dst, g))
                    link(dve.scalar_tensor_tensor(dst, srcs[c], rstd[:, u, c:c + 1], g, ALU.mult, ALU.mult))
                    dve.tensor_tensor(x[:, c, :], x[:, c, :], xhat[:, c, :], ALU.add).then_inc(x_done, 1)
                dve.wait_ge(x_done, TC * (q + 1))

            def head_lo(g, n):
                dve.wait_ge(oT_hi, n + 1)
                dve.tensor_tensor(hT_lo[:, 4 * g:4 * g + 4, :], ps[:, 4 * g:4 * g + 4, 0:T],
                                  hT_hi[:, 4 * g:4 * g + 4, :].bitcast(F32), ALU.subtract).then_inc(oT_lo, 1)

            dve.wait_ge(s_x, 16)
            rms(0, D)
            normalise(0)
            dve.wait_ge(rowsT, 1)
            dve.tensor_copy(cols[:, :, :], ps[:, 5, 0:DC * NROWS].rearrange("p (k r) -> p k r", k=DC)).then_inc(cols_ok, 1)
            dve.tensor_copy(lat_g[:, :], ps[:, 6, HR:HR + 3])
            dve.tensor_copy(ident_r[:, :], ident[:, :])
            dve.wait_ge(s_small, 48)
            link(dve.tensor_copy(pos_f[:, :], pos_i[:, :]))
            for c in range(TC):
                for s in range(2):
                    ins = dve.tensor_scalar(ang[:, s, c, :], ps[:, 6, 0:HR], pos_f[:, c:c + 1], None, ALU.mult)
            link(ins)
            for s, quarter in ((0, 0.25), (1, 0.0)):
                ins = dve.tensor_scalar(turns[:, s, :, :], ang[:, s, :, :], 1.0 / TWO_PI, quarter, ALU.mult, ALU.add)
            link(ins)
            link(dve.tensor_scalar(turns[:, :, :, :], turns[:, :, :, :], MAGIC, MAGIC, ALU.add, ALU.subtract))
            for part in (PI_A, PI_B, PI_C):
                flat = [a[:, :, :, :].rearrange("p s c f -> p (s c f)") for a in (ang, turns)]
                link(dve.scalar_tensor_tensor(flat[0], flat[1], -part, flat[0], ALU.mult, ALU.add))
            link(dve.tensor_scalar(ang[:, 0, :, :], ang[:, 0, :, :], TWO_PI / 4, None, ALU.add))
            dve.tensor_scalar(ang[:, :, :, :], ang[:, :, :, :], PI_MAX, -PI_MAX, ALU.min, ALU.max).then_inc(trig_a, 1)
            dve.wait_ge(cond_ok, 1)
            ada(DC)
            mod_cols(0)
            lo(0)
            ada(1)
            modulated(0)
            for m in range(1, 12):
                lo(m)
                ada(1)
            for h in range(0, SB_H, 2):
                dve.wait_ge(qkT_mm, h + 1)
                dve.tensor_copy(qkT[:, h, :], ps[:, h, :]).then_inc(qkT_d, 1)

            def flat_stick(g):
                return stick[g][:, :, :, :].rearrange("p h b n -> p h (b n)")

            ada(2)
            for g in range(2):
                dve.wait_ge(ln_ok, g + 1)
                dve.scalar_tensor_tensor(flat_stick(g), ps[:, 4 * g:4 * g + 4, 0:3 * P], 0.0, flat_stick(g),
                                         ALU.max, ALU.add).then_inc(sp_ok, 1)
            ada(2)
            M = first["sb_out"]
            lo(M)
            lo(M + 1)
            for g in range(2):
                head_lo(g, g)
            gate_rows(0, 0)
            lo(M + 2)
            lo(M + 3)
            mod_cols(1)
            residual(0, 1, [ps[:, 0:2, :], ps[:, 2:4, :]], 0)
            rms(2, D)
            normalise(2)
            lo(M + 4)
            modulated(1)
            lo(M + 5)
            ada(2)
            gate_rows(1, 1)
            M = first["gu"]

            def g_lo(j):
                dve.wait_ge(gThi, j + 1)
                dve.tensor_tensor(gT_lo[:, 2 * j:2 * j + 2, :], ps[:, 4 + j % 2, :].rearrange("p (a b) -> p a b", a=2),
                                  gT_hi[:, 2 * j:2 * j + 2, :].bitcast(F32), ALU.subtract).then_inc(gTlo, 1)

            for j in range(FG):
                lo(M + 2 * j + 2)
                if j >= 1:
                    g_lo(j - 1)
                if j + 1 == FG:
                    ada(1)
                lo(M + 2 * j + 3)
                dve.wait_ge(sil_ok, j + 1)
                dve.tensor_tensor(hid[j % 2][:, :, :], hid[j % 2][:, :, :], ps[:, 2 * (j % 2):2 * (j % 2) + 2, 256:512],
                                  ALU.mult).then_inc(hid_ok, 1)
                if j + 1 < FG:
                    ada(2 if j == 0 else 1)
            M = first["down"]
            ada(1)
            lo(M + 2)
            g_lo(FG - 1)
            ada(1)
            for d in range(3, FG):
                lo(M + d)
                ada(1)
            mod_cols(2)
            residual(1, 3, [ps[:, 0:2, :], ps[:, 2:4, :]], 1)
            rms(4, D)
            normalise(4)
            M = first["mla_in"]
            lo(M)
            modulated(2)
            lo(M + 1)
            gate_rows(2, 0)
            mod_cols(3)
            gate_rows(3, 1)
            lo(M + 2)
            rms(5, QL)
            rms(6, KVL)
            for c in range(TC):
                dve.tensor_scalar(lat[:, c, 0:QL], ps[:, c, 0:QL], rstd[:, 5, c:c + 1], None, ALU.mult)
                dve.tensor_scalar(lat[:, c, QL:QL + KVL], ps[:, c, QL:QL + KVL], rstd[:, 6, c:c + 1], None, ALU.mult)
                ins = dve.tensor_copy(kr[:, c, :], ps[:, c, QL + KVL:MLA_IN])
            ins.then_inc(lat_ok, 1)
            lo(M + 3)
            dve.wait_ge(lat_T, 1)
            for k in range(3):
                ins = dve.tensor_scalar(cT[:, k, :], ps[:, 2 + k // 2, (k % 2) * T:(k % 2 + 1) * T], lat_g[:, k:k + 1],
                                        None, ALU.mult)
            ins.then_inc(cT_ok, 1)
            dve.wait_ge(cThi, 1)
            dve.tensor_tensor(cT_lo[:, :, :], cT[:, :, :], cT_hi[:, :, :].bitcast(F32), ALU.subtract).then_inc(cTlo, 1)
            lo(M + 4)
            dve.wait_ge(trig_ok, 1)
            dve.wait_ge(lat_ok, 1)

            def rotate(x1, x2, cos, sin, t):
                dve.tensor_tensor(t[0], x1, cos, ALU.mult)
                dve.tensor_tensor(t[1], x2, sin, ALU.mult)
                dve.tensor_tensor(t[2], x2, cos, ALU.mult)
                link(dve.tensor_tensor(t[3], x1, sin, ALU.mult))
                dve.tensor_tensor(x1, t[0], t[1], ALU.subtract)
                return dve.tensor_tensor(x2, t[2], t[3], ALU.add)

            for c in range(TC):
                link(rotate(kr[:, c, 0:HR], kr[:, c, HR:ROPE], trig[:, 0, c, :], trig[:, 1, c, :],
                            [rt[:, n, 0, :] for n in range(4)]))
            dve.wait_ge(ev_q, 8)
            for c in range(TC):
                q = qn[:, c, :].rearrange("p (h w) -> p h w", h=MLA_H)
                cos, sin = (trig[:, s, c, :].unsqueeze(1).broadcast_to([P, MLA_H, HR]) for s in range(2))
                ins = rotate(q[:, :, NOPE:NOPE + HR], q[:, :, NOPE + HR:QW], cos, sin, [rt[:, n, :, :] for n in range(4)])
                if c + 1 < TC:
                    link(ins)
            ins.then_inc(rope_ok, 1)
            dve.wait_ge(kT_mm, 1)
            dve.tensor_copy(knT[:, :, :].rearrange("p (b a) t -> p b (a t)", b=4), ps[:, 0:4, :]).then_inc(kT_ok, 1)
            dve.wait_ge(rT_mm, 2)
            dve.tensor_copy(krT[:, :], ps[0:ROPE, 0, 0:T]).then_inc(rT_d, 1)
            for g in range(2):
                dve.wait_ge(s_mm, g + 1)
                sc = ps[:, 4 * g:4 * g + 4, 0:3 * P].rearrange("p h (b n) -> p h b n", b=3)
                dve.tensor_copy(prob[g][:, :, 1, :], sc[:, :, 1, :])
                link(dve.tensor_tensor(prob[g][:, :, 0, :], sc[:, :, 0, :],
                                       causal[:, :].unsqueeze(1).broadcast_to([P, 4, P]), ALU.add))
                link(dve.tensor_tensor(prob[g][:, :, 2, :], sc[:, :, 2, :],
                                       causal[:, :].unsqueeze(1).broadcast_to([P, 4, P]), ALU.add))
                dve.tensor_reduce(nmax[:, g, 0, :], prob[g][:, :, 0, :], AX.X, ALU.max, negate=True)
                dve.tensor_reduce(nmax[:, g, 1, :], prob[g][:, :, 1:3, :].rearrange("p h b n -> p h (b n)"), AX.X,
                                  ALU.max, negate=True).then_inc(smax_ok, 1)
            for g in range(2):
                dve.wait_ge(exp_ok, 8 * (g + 1))
                link(dve.reciprocal(rsum[:, g, :, :], psum_p[:, g, :, :]))
                dve.tensor_tensor(prob[g][:, :, 0, :], prob[g][:, :, 0, :],
                                  rsum[:, g, 0, :].unsqueeze(2).broadcast_to([P, 4, P]), ALU.mult)
                late = prob[g][:, :, 1:3, :].rearrange("p h b n -> p h (b n)")
                dve.tensor_tensor(late, late, rsum[:, g, 1, :].unsqueeze(2).broadcast_to([P, 4, 2 * P]),
                                  ALU.mult).then_inc(prob_ok, 1)
            for g in range(2):
                dve.wait_ge(pT_mm, g + 1)
                dve.tensor_copy(prob[g][:, :, :, :].rearrange("p h b n -> p h (b n)"),
                                ps[:, 4 * g:4 * g + 4, 0:3 * P]).then_inc(pT_ok, 1)
            for g in range(2):
                head_lo(g, 2 + g)
            M = first["mla_out"]
            for k in range(4):
                lo(M + k)
            residual(2, 7, [ps[:, 0:2, :], ps[:, 2:4, :]], 0)
            rms(8, D)
            normalise(8)
            dve.memset(macc[:, :, :], 0.0)
            dve.memset(spread[:, :].bitcast(F32), 0.0)
            dve.memset(ps[:, 4:6, :], 0.0).then_inc(e_blank, 1)
            modulated(3)
            dve.wait_ge(lg_mm, 1)
            link(dve.tensor_copy(lg[:, :, :], ps[:, 7, 0:TC * E].rearrange("p (c e) -> p c e", c=TC)))

            def best(logits, top, one):
                for c in range(TC):
                    link(dve.max(top[:, c, :], logits[:, c, :]))
                    link(dve.scalar_tensor_tensor(eq[:, c, :], logits[:, c, :], top[:, c, 0:1], eight[:, :],
                                                  ALU.is_equal, ALU.mult))
                    link(dve.max(kmax[:, c, :], eq[:, c, :]))
                    link(dve.tensor_scalar(one[:, c, :], eq[:, c, :], kmax[:, c, 0:1], None, ALU.is_equal))

            best(lg, top8, one1)
            link(dve.scalar_tensor_tensor(lg2[:, :, :].rearrange("p c e -> p (c e)"),
                                          one1[:, :, :].rearrange("p c e -> p (c e)"), NEG,
                                          lg[:, :, :].rearrange("p c e -> p (c e)"), ALU.mult, ALU.add))
            best(lg2, top8b, one2)
            dve.tensor_tensor(member[:, :, :], one1[:, :, :], one2[:, :, :], ALU.add).then_inc(member_ok, 1)
            dve.tensor_tensor(diff[:, :], top8b[:, :, 0], top8[:, :, 0], ALU.subtract).then_inc(wt_a, 1)
            dve.wait_ge(xs_hi, 1)
            dve.tensor_tensor(xhat_lo[:, :, :], xhat[:, :, :], xhat_hi[:, :, :].bitcast(F32), ALU.subtract)\
                .then_inc(xs_lo, 1)
            dve.wait_ge(wt_ok, 1)
            link(dve.tensor_scalar(wt[:, 0, :], wt[:, 1, :], 1.0, None, ALU.add))
            link(dve.reciprocal(wt[:, 0, :], wt[:, 0, :]))
            link(dve.tensor_tensor(wt[:, 1, :], wt[:, 1, :], wt[:, 0, :], ALU.mult))
            link(dve.memset(visit[:, :, :], 0.0))
            dve.wait_ge(pos_mm, 1)
            dve.wait_ge(member_ok, 1)
            for c in range(TC):
                where = ps[:, 7, 32 + c * E:32 + (c + 1) * E]
                dve.tensor_copy(visit[:, 0:E, 3 * c], where)
                dve.tensor_scalar(visit[:, E:2 * E, 3 * c], where, float(-CAP), None, ALU.add)
                link(dve.tensor_scalar(one1[:, c, :], one1[:, c, :], wt[:, 0, c:c + 1], None, ALU.mult))
                for r in range(2):
                    dve.tensor_copy(visit[:, E * r:E * (r + 1), 3 * c + 1], member[:, c, :])
                    ins = dve.scalar_tensor_tensor(visit[:, E * r + 1:E * (r + 1) + 1, 3 * c + 2], one2[:, c, :],
                                                   wt[:, 1, c:c + 1], one1[:, c, :], ALU.mult, ALU.add)
                link(ins)
            link(dve.tensor_reduce(count_f[:, :], ps[:, 7, 48:48 + E], AX.X, ALU.max))
            link(dve.tensor_scalar(count_f[:, :], count_f[:, :], float(CAP), float(E), ALU.is_gt, ALU.mult))
            dve.tensor_scalar(n_end[:, :], count_f[:, :], float(E), None, ALU.add).then_inc(visit_ok, 1)

            def picks(loop_link, i):
                loop_link(dve.tensor_copy(cur[:, :], visit[:, i, :]))
                for c in range(TC):
                    ins = dve.tensor_scalar(pick[:, c, :], slot_no[:, :], cur[:, 3 * c:3 * c + 1],
                                            cur[:, 3 * c + 1:3 * c + 2], ALU.is_equal, ALU.mult)
                ins.then_inc(e_pick, 1)

            def x_lo(n):
                for b in range(2):
                    dve.wait_ge(e_xhi, n + b + 1)
                    dve.tensor_tensor(xe_lo[:, 4 * b:4 * b + 4, :], xe32[:, 4 * b:4 * b + 4, :],
                                      xe_hi[:, 4 * b:4 * b + 4, :].bitcast(F32), ALU.subtract).then_inc(e_xlo, 1)

            def y_lo(n):
                dve.wait_ge(e_y, n)
                dve.tensor_tensor(ye_lo[:, :].rearrange("p (a b) -> p a b", a=2), ps[:, 4:6, :],
                                  ye_hi[:, :].bitcast(F32).rearrange("p (a b) -> p a b", a=2), ALU.subtract)\
                    .then_inc(e_ylo, 1)

            def collect(n, c):
                dve.wait_ge(e_sc, n)
                m = macc[:, c, :].rearrange("p (a b) -> p a b", a=2)
                dve.scalar_tensor_tensor(m, ps[:, 6:8, :], cur[:, 3 * c + 2:3 * c + 3], m, ALU.mult, ALU.add)\
                    .then_inc(e_add, 1)

            picks(link, 0)
            x_lo(0)
            last = dve.value_load(n_end[0:1, 0:1], min_val=E, max_val=2 * E)
            with dve.Fori(0, last) as i:
                def loop_link(ins):
                    ins.then_inc(e_step, 1)
                    dve.wait_ge(e_step, i + 1)

                def elo(k):
                    dve.wait_ge(hi_done, M0 + k + 1 + NK * i)
                    n_c = piece_elems(expert_piece(0, k)[1])
                    dve.tensor_tensor(m_lo[k % NB][:, 0:n_c], ring[(N0 + k) % R][:, 0:n_c],
                                      m_hi[k % NB][:, 0:n_c].bitcast(F32), ALU.subtract).then_inc(freed, 1)

                def eg_lo(j):
                    dve.wait_ge(e_ghi, EG * i + j + 1)
                    n_f = gw[j] // P
                    dve.tensor_tensor(eT_lo[:, 2 * j:2 * j + n_f, :].rearrange("p a b -> p (a b)"),
                                      ps[:, 2 + j % 2, 0:gw[j]],
                                      eT_hi[:, 2 * j:2 * j + n_f, :].bitcast(F32).rearrange("p a b -> p (a b)"),
                                      ALU.subtract).then_inc(e_glo, 1)

                elo(0)
                elo(1)
                elo(2)
                y_lo(i + 1)
                for j in range(EG):
                    elo(2 * j + 3)
                    if j >= 1:
                        eg_lo(j - 1)
                    dve.wait_ge(e_sil, EG * i + j + 1)
                    dve.tensor_tensor(ehid[j % 2][:, 0:gw[j]], esil[j % 2][:, 0:gw[j]],
                                      ps[:, j % 2, gw[j]:2 * gw[j]], ALU.mult).then_inc(e_hid, 1)
                    elo(2 * j + 4)
                    if j in (1, 2):
                        collect(2 * i + j, j - 1)
                    if j == 4:
                        dve.wait_ge(e_pT, i + 1)
                        picks(loop_link, i + 1)
                elo(2 * EG + 3)
                eg_lo(EG - 1)
                elo(2 * EG + 4)
                x_lo(2 * i + 2)
                elo(2 * EG + 5)
            y_lo(last + 1)
            collect(2 * last + 1, 0)
            collect(2 * last + 2, 1)
            dve.wait_ge(e_add, 2 * last + 2)
            residual(3, 9, [macc[:, 0, :], macc[:, 1, :]], 1)
            assert pieces[0] == N0

        @block.tensor
        def _(pe):
            def three(out, a_hi, a_lo, b_hi, b_lo, start, stop):
                pe.matmul(out, a_hi, b_lo, start=start, stop=False)
                pe.matmul(out, a_hi, b_hi, start=False, stop=False)
                return pe.matmul(out, a_lo, b_hi, start=False, stop=stop)

            def product(m, k0, groups, a_hi, a_lo, total):
                n = no_of[m]
                pe.wait_ge(freed, n + 1)
                shape = stream[n][3]
                kc, width = shape[0], piece_elems(shape[1:])
                bh = w_hi[m % 2][:, 0:kc * width].rearrange("p (k n) -> p k n", k=kc)
                bl = w_lo[m % 2][:, 0:kc * width].rearrange("p (k n) -> p k n", k=kc)
                for c in range(TC):
                    for c0, cn, out in groups:
                        for k in range(kc):
                            ins = three(out(c), a_hi[:, k0 + k, c * P:(c + 1) * P], a_lo[:, k0 + k, c * P:(c + 1) * P],
                                        bh[:, k, c0:c0 + cn], bl[:, k, c0:c0 + cn],
                                        k0 + k == 0, k0 + k == total - 1)
                ins.then_inc(used, 1)

            def transpose_xhat(v):
                pe.wait_ge(xhat_done, TC * (v + 1))
                for b in range(4):
                    for a in range(2):
                        for c in range(TC):
                            k = 2 * b + a
                            ins = pe.transpose(ps[:, b, a * T + c * P:a * T + (c + 1) * P],
                                               xhat[:, c, k * P:(k + 1) * P], ident[:, :])
                    ins.then_inc(tr_done, 1)

            def mod_columns(v):
                l, w = divmod(v, 2)
                for s in range(2):
                    for k in range(DC):
                        ins = pe.matmul(ps[:, 4, s * DC + k:s * DC + k + 1],
                                        acc[:, (3 * w + s) * D + k * P:(3 * w + s) * D + (k + 1) * P],
                                        ones[:, 0:1], start=True, stop=True)
                ins.then_inc(mod_mm, 1)

            def spread_row(out, r, a):
                return pe.matmul(out, ident[0:NROWS, r:r + 1].to_broadcast([NROWS, P]),
                                 rows[0:NROWS, a * 512:(a + 1) * 512], start=False, stop=True, skip_group_check=True)

            def gate_spread(l, w):
                s = 3 * w + 2
                for a in range(2):
                    pe.matmul(ps[:, 4 + a, :], ones[:, :], acc[:, s * D + a * 512:s * D + (a + 1) * 512],
                              start=True, stop=False)
                    pe.matmul(ps[:, 4 + a, :], ident[0:NROWS, 6 * l + s:6 * l + s + 1].to_broadcast([NROWS, P]),
                              rows[0:NROWS, a * 512:(a + 1) * 512], start=False, stop=True)
                for a in range(2):
                    r = 12 + 4 * l + 2 * w + 1
                    ins = pe.matmul(ps[:, 6 + a, :], ident[0:NROWS, r:r + 1].to_broadcast([NROWS, P]),
                                    rows[0:NROWS, a * 512:(a + 1) * 512], start=True, stop=True)
                ins.then_inc(gate_mm, 1)

            def ada_ready(l, thirds):
                pe.wait_ge(freed, ada_no[(l, thirds, DC - 1)] + 1)

            def bank(base_, step):
                return lambda c: ps[:, base_ + step * c, :]

            def out_product(name):
                M = first[name]
                for g in range(2):
                    for h in range(2):
                        product(M + 2 * g + h, 4 * h, [(0, 512, bank(g, 2))], hT_hi, hT_lo, DC)

            pe.wait_ge(idn, 1)
            pe.wait_ge(consts, 9)
            pe.wait_ge(s_rows, 16 * 8)
            for k in range(DC):
                pe.transpose(ps[:, 5, k * NROWS:(k + 1) * NROWS], rows[0:NROWS, k * P:(k + 1) * P],
                             ident[0:NROWS, 0:NROWS])
            pe.matmul(ps[:, 6, 0:HR], ones[0:1, :], freq[0:1, :], start=True, stop=True)
            pe.transpose(ps[:, 6, HR:HR + 3], lat_rows[0:3, :], ident[0:3, 0:3]).then_inc(rowsT, 1)
            transpose_xhat(0)
            ada_ready(0, 0)
            mod_columns(0)
            pe.wait_ge(hTlo, 4)
            for g in range(6):
                if g >= 4:
                    pe.wait_ge(ev_qkv, TC * (g - 3))
                for h in range(2):
                    product(2 * g + h, 4 * h, [(0, 512, bank(2 * (g % 4), 1))], hT_hi, hT_lo, DC)
            pe.wait_ge(ev_qkv, 12)
            for h in range(SB_H):
                for s in range(2):
                    for c in range(TC):
                        ins = pe.transpose(ps[:, h, s * T + c * P:s * T + (c + 1) * P],
                                           qkv[:, c, s * D + h * P:s * D + (h + 1) * P], ident[:, :])
                ins.then_inc(qkT_mm, 1)
            for g in range(2):
                pe.wait_ge(qkT_d, 2 * g + 2)
                pe.wait_ge(qkT_a, 2 * g + 2)
                for h in range(4 * g, 4 * g + 4):
                    pe.matmul(ps[:, h, 0:T], qkT[:, h, T:T + P], qkT[:, h, 0:T], start=True, stop=False,
                              skip_group_check=True)
                    ins = pe.matmul(ps[:, h, T:T + P], qkT[:, h, T + P:2 * T], qkT[:, h, P:T], start=False,
                                    stop=False, skip_group_check=True)
                ins.then_inc(z_mm, 1)
            for g in range(2):
                pe.wait_ge(sp_masked, 2 * g + 2)
                for h in range(4):
                    o, s = ps[:, 4 * g + h, :], stick[g][:, h, :, :].rearrange("p b n -> p (b n)")
                    pe.matmul(o[:, 0:T], neg_ge[:, :], s[:, 0:T], start=False, stop=False, skip_group_check=True)
                    pe.matmul(o[:, P:T], neg_one[:, :], s[:, T:T + P], start=False, stop=False, skip_group_check=True)
                    ins = pe.matmul(o[:, T:T + P], neg_ge[:, :], s[:, T:T + P], start=False, stop=True,
                                    skip_group_check=True)
                ins.then_inc(tail_mm, 1)

            def weighted_values(g, p, value):
                for h in range(4):
                    o, s = ps[:, 4 * g + h, :], p[g][:, h, :, :].rearrange("p b n -> p (b n)")
                    pe.matmul(o[:, 0:T], value(0, 4 * g + h), s[:, 0:T], start=True, stop=False, skip_group_check=True)
                    ins = pe.matmul(o[:, P:T], value(1, 4 * g + h), s[:, T:T + P], start=False, stop=True,
                                    skip_group_check=True)
                ins.then_inc(pv_mm, 1)

            for g in range(2):
                pe.wait_ge(a_masked, 2 * g + 2)
                weighted_values(g, stick, lambda c, h: qkv[:, c, 2 * D + h * P:2 * D + (h + 1) * P])
            ada_ready(0, 2)
            pe.wait_ge(oT_lo, 2)
            gate_spread(0, 0)
            out_product("sb_out")
            pe.wait_ge(gate_ok, 1)
            mod_columns(1)
            transpose_xhat(1)
            pe.wait_ge(mod_ok, 2)
            gate_spread(0, 1)
            pe.wait_ge(hTlo, 8)
            M = first["gu"]

            def turn_hidden(j):
                pe.wait_ge(hid_ok, j + 1)
                if j >= 2:
                    pe.wait_ge(gTlo, j - 1)
                else:
                    pe.wait_ge(gate_ok, 2)
                for a in range(2):
                    for c in range(TC):
                        ins = pe.transpose(ps[:, 4 + j % 2, a * T + c * P:a * T + (c + 1) * P],
                                           hid[j % 2][:, c, a * P:(a + 1) * P], ident[:, :])
                ins.then_inc(hid_T, 1)

            for j in range(FG):
                if j >= 2:
                    pe.wait_ge(hid_ok, j - 1)
                product(M + 2 * j, 0, [(0, 512, bank(2 * (j % 2), 1))], hT_hi, hT_lo, DC)
                if j >= 1:
                    turn_hidden(j - 1)
                product(M + 2 * j + 1, 4, [(0, 512, bank(2 * (j % 2), 1))], hT_hi, hT_lo, DC)
            M = first["down"]
            pe.wait_ge(hid_ok, FG)
            halves = [(0, 512, bank(0, 2)), (512, 512, bank(1, 2))]
            for d in range(FG):
                pe.wait_ge(gTlo, d + 1)
                product(M + d, 2 * d, halves, gT_hi, gT_lo, FC)
                if d == 0:
                    turn_hidden(FG - 1)
            ada_ready(1, 2)
            pe.wait_ge(gTlo, FG)
            mod_columns(2)
            pe.wait_ge(mod_ok, 3)
            gate_spread(1, 0)
            transpose_xhat(2)
            pe.wait_ge(gate_ok, 3)
            mod_columns(3)
            pe.wait_ge(mod_ok, 4)
            gate_spread(1, 1)
            M = first["mla_in"]
            pe.wait_ge(hTlo, 12)
            for h in range(2):
                product(M + h, 4 * h, [(0, MLA_IN, lambda c: ps[:, c, 0:MLA_IN])], hT_hi, hT_lo, DC)
            pe.wait_ge(lat_ok, 1)
            for k in range(3):
                for c in range(TC):
                    ins = pe.transpose(ps[:, 2 + k // 2, (k % 2) * T + c * P:(k % 2) * T + (c + 1) * P],
                                       lat[:, c, k * P:(k + 1) * P], ident[:, :])
            ins.then_inc(lat_T, 1)
            pe.wait_ge(cTlo, 1)
            pe.wait_ge(gate_ok, 4)
            for u in range(2):
                product(M + 2 + u, 0, [(s * 384, 384, lambda c, s=s, u=u: ps[:, 4 * (1 - u) + 2 * c + s, 0:384])
                                       for s in range(2)], cT_hi, cT_lo, 2)
            pe.wait_ge(ev_q, 8)
            n = no_of[M + 4]
            pe.wait_ge(freed, n + 1)
            for c in range(TC):
                for s in range(4):
                    ins = three(ps[:, 4 * c + s, :], cT_hi[:, 2, c * P:(c + 1) * P], cT_lo[:, 2, c * P:(c + 1) * P],
                                w_hi[(M + 4) % 2][:, s * 512:(s + 1) * 512], w_lo[(M + 4) % 2][:, s * 512:(s + 1) * 512],
                                True, True)
            ins.then_inc(used, 1)
            pe.wait_ge(ev_kv, 4)
            for h in range(MLA_H):
                for c in range(TC):
                    ins = pe.transpose(ps[:, 4 + h // 2, (h % 2) * T + c * P:(h % 2) * T + (c + 1) * P],
                                       qn[:, c, h * QW:h * QW + NOPE], ident[:, :])
            ins.then_inc(qT_mm, 1)
            pe.wait_ge(ev_kv, 8)
            for h in range(MLA_H):
                for c in range(TC):
                    ins = pe.transpose(ps[:, h // 2, (h % 2) * T + c * P:(h % 2) * T + (c + 1) * P],
                                       kvn[:, c, h * KVW:h * KVW + NOPE], ident[:, :])
            ins.then_inc(kT_mm, 1)
            pe.wait_ge(qT_ok, 1)
            pe.wait_ge(rope_ok, 1)
            for h in range(MLA_H):
                for c in range(TC):
                    ins = pe.transpose(ps[0:ROPE, 4 + h // 2, (h % 2) * T + c * P:(h % 2) * T + (c + 1) * P],
                                       qn[:, c, h * QW + NOPE:(h + 1) * QW], ident[:, :])
            ins.then_inc(rT_mm, 1)
            pe.wait_ge(kT_ok, 1)
            for c in range(TC):
                ins = pe.transpose(ps[0:ROPE, 0, c * P:(c + 1) * P], kr[:, c, :], ident[:, :])
            ins.then_inc(rT_mm, 1)
            pe.wait_ge(rT_d, 1)
            pe.wait_ge(rT_a, 1)
            for g in range(2):
                for h in range(4 * g, 4 * g + 4):
                    for q0, o, keys in ((0, ps[:, h, 0:P], P), (P, ps[:, h, P:3 * P], T)):
                        pe.matmul(o, qnT[:, h, q0:q0 + P], knT[:, h, 0:keys], start=True, stop=False)
                        ins = pe.matmul(o, qrT[:, h, q0:q0 + P], krT[:, 0:keys], start=False, stop=True)
                ins.then_inc(s_mm, 1)
            for g in range(2):
                pe.wait_ge(prob_ok, g + 1)
                for h in range(4):
                    for b in range(3):
                        ins = pe.transpose(ps[:, 4 * g + h, b * P:(b + 1) * P], prob[g][:, h, b, :], ident[:, :])
                ins.then_inc(pT_mm, 1)
            for g in range(2):
                pe.wait_ge(pT_ok, g + 1)
                weighted_values(g, prob, lambda c, h: kvn[:, c, h * KVW + NOPE:(h + 1) * KVW])
            pe.wait_ge(oT_lo, 4)
            out_product("mla_out")
            transpose_xhat(3)
            pe.wait_ge(hTlo, 16)
            pe.wait_ge(s_small, 48)
            for c in range(TC):
                o = ps[:, 7, c * E:(c + 1) * E]
                pe.matmul(o, ones[0:1, :], br[0:1, :], start=True, stop=False)
                for k in range(DC):
                    for half in (hT_lo, hT_hi):
                        ins = pe.matmul(o, half[:, k, c * P:(c + 1) * P].bitcast(F32), wr[:, k, :], start=False,
                                        stop=(k == DC - 1 and half is hT_hi))
            ins.then_inc(lg_mm, 1)
            pe.wait_ge(member_ok, 1)
            for c in range(TC):
                o = ps[:, 7, 32 + c * E:32 + (c + 1) * E]
                if c:
                    pe.matmul(o, ones[:, :], member[:, 0, :], start=True, stop=False)
                pe.matmul(o, before[:, :], member[:, c, :], start=(c == 0), stop=True)
            for c in range(TC):
                ins = pe.matmul(ps[:, 7, 48:48 + E], ones[:, :], member[:, c, :], start=(c == 0), stop=(c == TC - 1))
            ins.then_inc(pos_mm, 1)

            def gather(visit_no):
                pe.wait_ge(e_pick, visit_no + 1)
                for b in range(2):
                    for a in range(4):
                        k = 4 * b + a
                        for c in range(TC):
                            for half in (xhat_hi, xhat_lo):
                                ins = pe.matmul(ps[:, b, a * P:(a + 1) * P], half[:, c, k * P:(k + 1) * P],
                                                pick[:, c, :], start=(c == 0 and half is xhat_hi),
                                                stop=(c == TC - 1 and half is xhat_lo))
                    ins.then_inc(e_gath, 1)

            def scatter(c):
                for a in range(2):
                    for half in (ye_hi, ye_lo):
                        ins = pe.matmul(ps[:, 6 + a, :], spread[:, c * P:(c + 1) * P], half[:, a * 512:(a + 1) * 512],
                                        start=(half is ye_hi), stop=(half is ye_lo))
                ins.then_inc(e_sc, 1)

            pe.wait_ge(xs_lo, 1)
            gather(0)
            pe.wait_ge(visit_ok, 1)
            last = pe.value_load(n_end[0:1, 0:1], min_val=E, max_val=2 * E)
            with pe.Fori(0, last) as i:
                def expert_product(k, kc, lhs_hi, lhs_lo, k0, outs, total_k):
                    pe.wait_ge(freed, N0 + k + 1 + NK * i)
                    n_c = piece_elems(expert_piece(0, k)[1])
                    bh = m_hi[k % NB][:, 0:n_c].rearrange("p (k n) -> p k n", k=kc)
                    bl = m_lo[k % NB][:, 0:n_c].rearrange("p (k n) -> p k n", k=kc)
                    for c0, cn, out in outs:
                        for q in range(kc):
                            ins = three(out, lhs_hi[:, k0 + q, :], lhs_lo[:, k0 + q, :], bh[:, q, c0:c0 + cn],
                                        bl[:, q, c0:c0 + cn], k0 + q == 0, k0 + q == total_k - 1)
                    ins.then_inc(used, 1)

                def turn(j):
                    pe.wait_ge(e_hid, EG * i + j + 1)
                    if j >= 2:
                        pe.wait_ge(e_glo, EG * i + j - 1)
                    for a in range(gw[j] // P):
                        ins = pe.transpose(ps[:, 2 + j % 2, a * P:(a + 1) * P], ehid[j % 2][:, a * P:(a + 1) * P],
                                           ident[:, :])
                    ins.then_inc(e_hidT, 1)

                pe.wait_ge(e_xlo, 2 * i + 2)
                for j in range(EG):
                    if j >= 2:
                        pe.wait_ge(e_hid, EG * i + j - 1)
                    outs = [(0, 2 * gw[j], ps[:, j % 2, 0:2 * gw[j]])]
                    expert_product(2 * j, 4, xe_hi, xe_lo, 0, outs, DC)
                    if j >= 1:
                        turn(j - 1)
                    if j == 4:
                        pe.wait_ge(e_add, 2 * i + 2)
                        pe.wait_ge(e_pick, i + 1)
                        for c in range(TC):
                            ins = pe.matmul(ps[:, 6, c * P:(c + 1) * P], pick[:, c, :], ident_r[:, :], start=True,
                                            stop=True)
                        ins.then_inc(e_pT, 1)
                    expert_product(2 * j + 1, 4, xe_hi, xe_lo, 4, outs, DC)
                    if j == 1:
                        pe.wait_ge(e_ylo, i + 1)
                        scatter(0)
                    if j == 2:
                        pe.wait_ge(e_add, 2 * i + 1)
                        scatter(1)
                for d in range(EG):
                    pe.wait_ge(e_glo, EG * i + d + 1)
                    outs = [(a * 512, 512, ps[:, 4 + a, :]) for a in range(2)]
                    expert_product(2 * EG + d, dk[d], eT_hi, eT_lo, 2 * d, outs, EFC)
                    if d == 0:
                        turn(EG - 1)
                    if d == 1:
                        gather(i + 1)
            pe.wait_ge(e_ylo, last + 1)
            scatter(0)
            pe.wait_ge(e_add, 2 * last + 1)
            scatter(1)


def kernel(**inputs):
    import numpy as np
    import concourse.bacc as bacc
    from concourse.bass_utils import run_bass_kernel_spmd as run

    nc = bacc.Bacc("TRN2", target_bir_lowering=False, num_devices=1)
    arrays, args = {}, []

    def given(name, a):
        a = np.ascontiguousarray(a)
        arrays["in_" + name] = a
        args.append(nc.dram_tensor("in_" + name, a.shape, mybir.dt.from_np(a.dtype), kind="ExternalInput").ap())

    for name in ("x", "c", "positions", "ada_w", "ada_b", "norm_g", "sb_w_in", "sb_w_out", "mla_w_in", "mla_g_q",
                 "mla_w_q_up", "mla_g_kv", "mla_w_kv_up", "mla_w_out", "ffn_w_gu", "ffn_w_down", "moe_w_router",
                 "moe_b_router", "moe_w_gu", "moe_w_down"):
        given(name, inputs[name])
    given("inv_freq", (np.float32(500000.0) ** (-np.arange(0, ROPE, 2, dtype=np.float32) / np.float32(ROPE)))
          .astype(np.float32)[None, :])
    out = nc.dram_tensor("out", (1, T, D), F32, kind="ExternalOutput").ap()
    trunk(nc, *args, out)
    return run(nc, [arrays], core_ids=[0]).results[0]["out"]
```

```python
from contextlib import ExitStack

import concourse.bass as bass
from concourse import mybir

F32 = mybir.dt.float32
F32R = mybir.dt.float32r
I32 = mybir.dt.int32
ALU = mybir.AluOpType
ACT = mybir.ActivationFunctionType
AX = mybir.AxisListType

P = 128
T = 256
TC = T // P
D = 1024
DC = D // P
EPS = 1e-6
SB_H = 8
FF = 2816
FG = FF // 256
FC = FF // P
MLA_H = 8
QL, KVL, NOPE, ROPE = 256, 128, 128, 64
HR = ROPE // 2
MLA_IN = QL + KVL + ROPE
QW = NOPE + ROPE
KVW = 2 * P
E = 8
EF = 1408
EFC = EF // P
EG = (EFC + 1) // 2
CAP = P
R = 6
PIECE = 2048
NEG = -1.0e30
MAGIC = 12582912.0
TWO_PI = 6.283185307179586
PI_A, PI_B = 6.28125, 0.0019350051879882812
PI_C = TWO_PI - PI_A - PI_B
PI_MAX = 3.1415925

COND_ROW = 20
NROWS = 21


def trunk(nc, x_d, c_d, pos_d, ada_w, ada_b, norm_g, sb_w_in, sb_w_out, mla_w_in, mla_g_q, mla_w_q_up,
          mla_g_kv, mla_w_kv_up, mla_w_out, ffn_w_gu, ffn_w_down, w_router, b_router, moe_w_gu,
          moe_w_down, inv_freq, out_d):
    stream = []
    weight_no = {}
    first = {}

    def rows_view(w, k0, k, c0, c):
        return w.rearrange("(k p) n -> p k n", p=P)[:, k0:k0 + k, c0:c0 + c]

    def gate_up_view(w, k0, k, c0, c):
        return w.rearrange("(k p) (s n) -> p k s n", p=P, s=2)[:, k0:k0 + k, :, c0:c0 + c]

    def add_ada(layer, third, k):
        stream.append(("ada", (layer, third, k), ada_w[layer][k * P:(k + 1) * P, third * 2048:third * 2048 + 2048],
                       (2048,)))

    def add_weight(name, src, shape):
        first.setdefault(name, len(weight_no))
        weight_no[len(stream)] = len(weight_no)
        stream.append(("weight", name, src, shape))

    for k in range(DC):
        add_ada(0, 0, k)
    ada0 = [(t, k) for t in (1, 2) for k in range(DC)]
    for g in range(6):
        for h in range(2):
            add_weight("qkv", rows_view(sb_w_in[0], 4 * h, 4, g * 512, 512), (4, 512))
            if g < 5:
                add_ada(0, *ada0.pop(0))
    for n, (h, g) in enumerate(((1, 0), (1, 1), (0, 0), (0, 1))):
        add_weight("sb_out", rows_view(sb_w_out[0], 4 * h, 4, g * 512, 512), (4, 512))
        for _ in range((0, 4, 1, 1)[n]):
            add_ada(0, *ada0.pop(0))
    assert not ada0
    ada1 = [(t, k) for t in range(3) for k in range(DC)]
    for j in range(FG):
        add_weight("gu", gate_up_view(ffn_w_gu[0], 0, 4, j * 256, 256), (4, 2, 256))
        add_weight("gu", gate_up_view(ffn_w_gu[0], 4, 4, j * 256, 256), (4, 2, 256))
        for _ in range(2 if j < 2 else 1):
            add_ada(1, *ada1.pop(0))
    for d in range(FG):
        add_weight("down", rows_view(ffn_w_down[0], 2 * d, 2, 0, D), (2, D))
        add_ada(1, *ada1.pop(0))
    assert not ada1
    for h in range(2):
        add_weight("mla_in", rows_view(mla_w_in[0], 4 * h, 4, 0, MLA_IN), (4, MLA_IN))
    for u in range(2):
        add_weight("q_up", rows_view(mla_w_q_up[0], 0, 2, u * 768, 768), (2, 768))
    add_weight("kv_up", rows_view(mla_w_kv_up[0], 0, 1, 0, 2048), (1, 2048))
    for g in range(2):
        for h in range(2):
            add_weight("mla_out", rows_view(mla_w_out[0], 4 * h, 4, g * 512, 512), (4, 512))
    N0, M0 = len(stream), len(weight_no)
    no_of = {m: n for n, m in weight_no.items()}
    ada_no = {p[1]: n for n, p in enumerate(stream) if p[0] == "ada"}
    NK = 3 * EG
    assert NK % R == 0 and NK % 3 == 0
    gw = [min(2, EFC - 2 * j) * P for j in range(EG)]
    dk = [min(2, EFC - 2 * d) for d in range(EG)]

    def expert_piece(e, k):
        if k < 2 * EG:
            j, h = divmod(k, 2)
            w = moe_w_gu[0, e].rearrange("(k p) (s n) -> p k s n", p=P, s=2)
            return w[:, 4 * h:4 * h + 4, :, j * 256:j * 256 + gw[j]], (4, 2, gw[j])
        d = k - 2 * EG
        w = moe_w_down[0, e].rearrange("(k p) n -> p k n", p=P)
        return w[:, 2 * d:2 * d + dk[d], :], (dk[d], D)

    def piece_elems(shape):
        n = 1
        for s in shape:
            n *= s
        return n

    ctx = ExitStack()
    with ctx:
        cursor = [(nc.sbuf_base + 63) // 32 * 32]

        def sb(name, shape, dt=F32, at=None):
            if at is None:
                at = cursor[0]
                cursor[0] += (4 * piece_elems(shape[1:]) + 31) // 32 * 32
            return nc.alloc_sbuf_tensor_at(name, shape, dt, offset=at)

        ring = [sb(f"ring{r}", [P, PIECE]) for r in range(R)]
        w_hi = [sb(f"w_hi{b}", [P, PIECE], F32R) for b in range(2)]
        w_lo = [sb(f"w_lo{b}", [P, PIECE], F32R) for b in range(2)]
        x = sb("x", [P, TC, D])
        xhat_at = cursor[0]
        xhat = sb("xhat", [P, TC, D])
        hT_at = cursor[0]
        hT_hi = sb("hT_hi", [P, DC, T], F32R)
        hT_lo = sb("hT_lo", [P, DC, T], F32R)
        gate = [sb(f"gate{w}", [P, D]) for w in range(2)]
        rows = sb("rows", [NROWS, D])
        ident = sb("ident", [P, P])
        ident_r = sb("ident_r", [P, P], F32R)
        ones = sb("ones", [P, P])
        neg_ge = sb("neg_ge", [P, P])
        neg_one = sb("neg_one", [P, P])
        before = sb("before", [P, P])
        causal = sb("causal", [P, P])
        slot_no = sb("slot_no", [P, P])
        cols = sb("cols", [P, DC, NROWS])
        lat_rows = sb("lat_rows", [3, P])
        lat_g = sb("lat_g", [P, 3])
        cond = sb("cond", [P, DC])
        shift = sb("shift", [P, 4, DC])
        scale = sb("scale", [P, 4, DC])
        ssq = sb("ssq", [P, 10, TC])
        rstd = sb("rstd", [P, 10, TC])
        warm_out = sb("warm_out", [1, 16])
        freq = sb("freq", [1, HR])
        pos_i = sb("pos_i", [P, TC], I32)
        pos_f = sb("pos_f", [P, TC])
        ang = sb("ang", [P, 2, TC, HR])
        turns = sb("turns", [P, 2, TC, HR])
        trig = sb("trig", [P, 2, TC, HR])
        wr = sb("wr", [P, DC, E])
        wr_hi = sb("wr_hi", [P, DC, E], F32R)
        wr_lo = sb("wr_lo", [P, DC, E], F32R)
        br = sb("br", [E, 1])
        lg = sb("lg", [P, TC, E])
        top8 = sb("top8", [P, TC, 8])
        eq = sb("eq", [P, TC, E])
        eight = sb("eight", [P, E])
        kmax = sb("kmax", [P, TC, 8])
        one1 = sb("one1", [P, TC, E])
        one2 = sb("one2", [P, TC, E])
        lg2 = sb("lg2", [P, TC, E])
        top8b = sb("top8b", [P, TC, 8])
        diff = sb("diff", [P, TC])
        wt = sb("wt", [P, 2, TC])
        member = sb("member", [P, TC, E])
        NV = 2 * E + 1
        visit = sb("visit", [P, NV, 3 * TC])
        cur = sb("cur", [P, 3 * TC])
        count_f = sb("count_f", [P, 1])
        n_end = sb("n_end", [P, 1], I32)
        acc_at = cursor[0]
        acc = sb("acc", [P, 6 * D])
        base = cursor[0]

        t32 = sb("t32", [P, DC, T], at=base + 36864)
        junk = sb("junk", [P, D], at=base)
        v0 = sb("v0", [P, TC, D], at=base)
        qkT = sb("qkT", [P, SB_H, 2 * T], at=base + 8192)
        stick = [sb(f"stick{g}", [P, 4, 3, P], at=base + 24576 + 6144 * g) for g in range(2)]
        gT_hi = sb("gT_hi", [P, FC, T], F32R, at=base)
        gT_lo = sb("gT_lo", [P, FC, T], F32R, at=base + 22528)
        hid = [sb(f"hid{b}", [P, 2, T], at=xhat_at + 2048 * b) for b in range(2)]
        qn = sb("qn", [P, TC, MLA_H * QW], at=base)
        kvn = sb("kvn", [P, TC, MLA_H * KVW], at=base + 12288)
        lat = sb("lat", [P, TC, QL + KVL], at=base + 28672)
        kr = sb("kr", [P, TC, ROPE], at=base + 31744)
        cT = sb("cT", [P, 3, T], at=base + 32256)
        cT_hi = sb("cT_hi", [P, 3, T], F32R, at=base + 35328)
        cT_lo = sb("cT_lo", [P, 3, T], F32R, at=base + 38400)
        krT = sb("krT", [ROPE, T], at=base + 41472)
        rt = sb("rt", [P, 4, MLA_H, HR], at=xhat_at)
        prob0 = sb("prob0", [P, 4, 3, P], at=base + 35328)
        prob1 = sb("prob1", [P, 4, 3, P], at=base + 28672)
        prob = [prob0, prob1]
        qnT = sb("qnT", [P, MLA_H, T], at=hT_at)
        knT = sb("knT", [P, MLA_H, T], at=hT_at + 8192)
        qrT = sb("qrT", [ROPE, MLA_H, T], at=acc_at)
        nmax = sb("nmax", [P, 2, TC, 4], at=base + 42496)
        psum_p = sb("psum_p", [P, 2, TC, 4], at=base + 42560)
        rsum = sb("rsum", [P, 2, TC, 4], at=base + 42624)
        macc = sb("macc", [P, TC, D], at=base)
        xe32 = sb("xe32", [P, DC, P], at=base + 8192)
        xe_hi = sb("xe_hi", [P, DC, P], F32R, at=base + 12288)
        xe_lo = sb("xe_lo", [P, DC, P], F32R, at=base + 16384)
        eT_hi = sb("eT_hi", [P, EFC, P], F32R, at=base + 20480)
        eT_lo = sb("eT_lo", [P, EFC, P], F32R, at=base + 26112)
        esil = [sb(f"esil{b}", [P, 256], at=base + 31744 + 1024 * b) for b in range(2)]
        ehid = [sb(f"ehid{b}", [P, 256], at=base + 33792 + 1024 * b) for b in range(2)]
        ye_hi = sb("ye_hi", [P, D], F32R, at=base + 35840)
        ye_lo = sb("ye_lo", [P, D], F32R, at=base + 39936)
        lgT = sb("lgT", [E, T], at=acc_at + 2048)
        pick = sb("pick", [P, TC, P], F32R, at=acc_at)
        spread = sb("spread", [P, T], F32R, at=acc_at + 1024)
        mjunk = sb("mjunk", [P, D], at=acc_at + 4096)
        NB = 3
        m_hi = w_hi + [sb("m_hi2", [P, PIECE], F32R, at=acc_at + 8192)]
        m_lo = w_lo + [sb("m_lo2", [P, PIECE], F32R, at=acc_at + 16384)]
        xhat_hi = sb("xhat_hi", [P, TC, D], F32R, at=hT_at)
        xhat_lo = sb("xhat_lo", [P, TC, D], F32R, at=hT_at + 8192)
        assert base + 45056 <= nc.sbuf_usable_end, (base, nc.sbuf_usable_end)

        ps = ctx.enter_context(nc.psum_tensor("ps", [P, 8, 512], F32))

        def sem(name):
            return ctx.enter_context(nc.semaphore(name))

        landed = [sem(f"landed{r}") for r in range(R)]
        s_x, s_rows, s_small, s_out = sem("s_x"), sem("s_rows"), sem("s_small"), sem("s_out")
        freed = sem("freed")
        hi_done = sem("hi_done")
        used = sem("used")
        consts, idn = sem("consts"), sem("idn")
        s_lat = sem("s_lat")
        c0_done = sem("c0_done")
        freqT, freq_ok = sem("freqT"), sem("freq_ok")
        rowsT = sem("rowsT")
        cols_ok = sem("cols_ok")
        cond_ok = sem("cond_ok")
        mod_mm, mod_ok = sem("mod_mm"), sem("mod_ok")
        gate_mm, gain_ok, gate_ok = sem("gate_mm"), sem("gain_ok"), sem("gate_ok")
        ss_done, var_done, root_done = sem("ss_done"), sem("var_done"), sem("root_done")
        rstd_done = sem("rstd_done")
        x_done = sem("x_done")
        xhat_done = sem("xhat_done")
        tr_done = sem("tr_done")
        t_done, hThi, hTlo = sem("t_done"), sem("hThi"), sem("hTlo")
        ev_qkv = sem("ev_qkv")
        z_mm, ln_ok, sp_ok = sem("z_mm"), sem("ln_ok"), sem("sp_ok")
        sp_masked, tail_mm, a_ok, a_masked, pv_mm = (sem("sp_masked"), sem("tail_mm"), sem("a_ok"),
                                                     sem("a_masked"), sem("pv_mm"))
        oT_hi, oT_lo = sem("oT_hi"), sem("oT_lo")
        sil_ok, hid_ok = sem("sil_ok"), sem("hid_ok")
        gThi, gTlo = sem("gThi"), sem("gTlo")
        trig_a, trig_ok = sem("trig_a"), sem("trig_ok")
        lat_ok, lat_T, cT_ok, cThi, cTlo = sem("lat_ok"), sem("lat_T"), sem("cT_ok"), sem("cThi"), sem("cTlo")
        ev_q, ev_kv, rope_ok = sem("ev_q"), sem("ev_kv"), sem("rope_ok")
        qT_mm, qT_ok, kT_mm, kT_ok = sem("qT_mm"), sem("qT_ok"), sem("kT_mm"), sem("kT_ok")
        rT_mm, rT_a, rT_d = sem("rT_mm"), sem("rT_a"), sem("rT_d")
        s_mm, smax_ok, exp_ok, prob_ok, pT_mm, pT_ok = (sem("s_mm"), sem("smax_ok"), sem("exp_ok"),
                                                        sem("prob_ok"), sem("pT_mm"), sem("pT_ok"))
        lg_mm, wt_a, wt_ok, member_ok, pos_mm, visit_ok = (sem("lg_mm"), sem("wt_a"), sem("wt_ok"),
                                                           sem("member_ok"), sem("pos_mm"), sem("visit_ok"))
        visit_0 = sem("visit_0")
        wr_cut, lgT_mm, lgT_ok = sem("wr_cut"), sem("lgT_mm"), sem("lgT_ok")
        dve_step, act_step = sem("dve_step"), sem("act_step")
        e_step = sem("e_step")
        e_pick, e_gath, e_t, e_xhi, e_xlo = sem("e_pick"), sem("e_gath"), sem("e_t"), sem("e_xhi"), sem("e_xlo")
        e_sil, e_hid, e_hidT, e_ghi, e_glo = (sem("e_sil"), sem("e_hid"), sem("e_hidT"), sem("e_ghi"),
                                              sem("e_glo"))
        e_y, e_ylo, e_sc, e_add, e_pT, e_blank = (sem("e_y"), sem("e_ylo"), sem("e_sc"), sem("e_add"),
                                                  sem("e_pT"), sem("e_blank"))
        xs_hi, xs_lo = sem("xs_hi"), sem("xs_lo")

        filled, total = [], [0] * R
        for n in range(N0 + NK):
            shape = stream[n][3] if n < N0 else expert_piece(0, n - N0)[1]
            total[n % R] += 16 * (2 if len(shape) == 3 else 1)
            filled.append(total[n % R])
        before_visits = [max([filled[n] for n in range(r, N0, R)]) for r in range(R)]
        per_visit = [total[r] - before_visits[r] for r in range(R)]

        def wait_piece(eng, n):
            eng.wait_ge(landed[n % R], filled[n])

        def wait_expert_piece(eng, i, k):
            n = N0 + k
            eng.wait_ge(landed[n % R], filled[n] + per_visit[n % R] * i)

        def slot(n, shape):
            return ring[n % R][:, 0:piece_elems(shape)]

        def load(eng, n, src, shape):
            dst = slot(n, shape)
            if len(shape) == 3:
                dst = dst.rearrange("p (k s n) -> p k s n", k=shape[0], s=shape[1])
                for s in range(2):
                    eng.dma_start(dst[:, :, s, :], src[:, :, s, :]).then_inc(landed[n % R], 16)
            elif len(shape) == 2:
                eng.dma_start(dst.rearrange("p (k n) -> p k n", k=shape[0]), src).then_inc(landed[n % R], 16)
            else:
                eng.dma_start(dst, src).then_inc(landed[n % R], 16)

        def chain(eng, step_sem):
            count = [0]

            def link(ins):
                ins.then_inc(step_sem, 1)
                count[0] += 1
                eng.wait_ge(step_sem, count[0])
            return link

        block = ctx.enter_context(nc.Block())

        @block.sync
        def _(sp):
            sp.dma_start(rows[COND_ROW:NROWS, :], c_d).then_inc(s_rows, 16)
            sp.dma_start(rows[0:12, :], ada_b.rearrange("l (s n) -> (l s) n", s=6)).then_inc(s_rows, 16)
            sp.dma_start(rows[12:20, :], norm_g.rearrange("l s n -> (l s) n")).then_inc(s_rows, 16)
            for n, (_, _, src, shape) in enumerate(stream):
                if n >= R:
                    sp.wait_ge(freed, n - R + 1)
                load(sp, n, src, shape)

            def visit_experts(lo, hi):
                with sp.Fori(lo, hi) as i:
                    for k in range(NK):
                        sp.wait_ge(freed, N0 + k - R + 1 + NK * i)
                        src, shape = expert_piece(i - lo, k)
                        load(sp, N0 + k, src, shape)

            visit_experts(0, E)
            sp.wait_ge(visit_ok, 1)
            last = sp.value_load(n_end[0:1, 0:1], min_val=E, max_val=2 * E)
            with sp.If(last > E):
                visit_experts(E, 2 * E)

        @block.gpsimd
        def _(pool):
            pool.memset(ones[:, :], 1.0).then_inc(consts, 1)
            pool.memset(neg_one[:, :], -1.0).then_inc(consts, 1)
            pool.memset(causal[:, :], 0.0).then_inc(consts, 1)
            pool.memset(ident[:, :], 0.0).then_inc(consts, 1)
            pool.iota(slot_no[:, :], pattern=[[1, P]], base=0, channel_multiplier=0,
                      allow_small_or_imprecise_dtypes=True).then_inc(consts, 1)
            pool.iota(eight[:, :], pattern=[[-1, E]], base=E, channel_multiplier=0,
                      allow_small_or_imprecise_dtypes=True).then_inc(consts, 1)
            pool.wait_ge(consts, 6)
            pool.affine_select(out=ident[:, :], in_=ident[:, :], compare_op=ALU.not_equal, fill=1.0, base=0,
                               pattern=[[-1, P]], channel_multiplier=1).then_inc(idn, 1)
            pool.affine_select(out=neg_ge[:, :], in_=neg_one[:, :], compare_op=ALU.is_ge, fill=0.0, base=0,
                               pattern=[[-1, P]], channel_multiplier=1).then_inc(consts, 1)
            pool.affine_select(out=before[:, :], in_=ones[:, :], compare_op=ALU.is_gt, fill=0.0, base=0,
                               pattern=[[1, P]], channel_multiplier=-1).then_inc(consts, 1)
            pool.affine_select(out=causal[:, :], in_=causal[:, :], compare_op=ALU.is_ge, fill=NEG, base=0,
                               pattern=[[-1, P]], channel_multiplier=1).then_inc(consts, 1)
            for n, g in enumerate((1, 0)):
                for ready, masked in ((sp_ok, sp_masked), (a_ok, a_masked)):
                    pool.wait_ge(ready, n + 1)
                    for b in (0, 2):
                        pool.affine_select(out=stick[g][:, :, b, :], in_=stick[g][:, :, b, :], compare_op=ALU.is_gt,
                                           fill=0.0, base=0, pattern=[[0, 4], [1, P]], channel_multiplier=-1)\
                            .then_inc(masked, 1)

        @block.scalar
        def _(act):
            link = chain(act, act_step)
            act.dma_start(x[:, :, :], x_d[0].rearrange("(c p) n -> p c n", p=P)).then_inc(s_x, 16)
            act.dma_start(lat_rows[0:2, :], mla_g_q[0].rearrange("(k n) -> k n", n=P)).then_inc(s_lat, 16)
            act.dma_start(lat_rows[2:3, :], mla_g_kv).then_inc(s_lat, 16)
            act.dma_start(freq[:, :], inv_freq).then_inc(s_lat, 16)
            act.dma_start(pos_i[:, :], pos_d[0].rearrange("(c p) -> p c", p=P),
                          allow_slow_non_contiguous=True).then_inc(s_small, 16)
            act.dma_start(wr[:, :, :], w_router[0].rearrange("(k p) n -> p k n", p=P)).then_inc(s_small, 16)
            act.dma_start(br[:, :], b_router.rearrange("o e -> e o"), allow_slow_non_contiguous=True)\
                .then_inc(s_small, 16)

            def hi(m):
                n = no_of[m]
                wait_piece(act, n)
                if m >= 2:
                    act.wait_ge(used, m - 1)
                cols_n = piece_elems(stream[n][3])
                act.activation(w_hi[m % 2][:, 0:cols_n], ring[n % R][:, 0:cols_n], ACT.Copy).then_inc(hi_done, 1)

            def squares(u, c, src, out=junk):
                if TC * u + c:
                    act.wait_ge(ss_done, TC * u + c)
                dst = out[:, 0:piece_elems(src.shape[1:])]
                if len(src.shape) == 3:
                    dst = dst.rearrange("p (a b) -> p a b", a=src.shape[1])
                act.activation(dst, src, ACT.Square, accum_out=ssq[:, u, c:c + 1]).then_inc(ss_done, 1)

            def root(u, c):
                act.wait_ge(var_done, TC * u + c + 1)
                act.activation(rstd[:, u, c:c + 1], ssq[:, u, c:c + 1], ACT.Sqrt).then_inc(root_done, 1)

            def branch_squares(u, q, b0, m, out=junk):
                for c in range(TC):
                    if c == 0:
                        act.wait_ge(c0_done, (q + 1) // 2 if q < 7 else 3)
                    else:
                        act.wait_ge(used, m + 1)
                    squares(q, c, ps[:, b0 + 2 * c:b0 + 2 * c + 2, :], out)
                    root(q, c)
                for c in range(TC):
                    act.wait_ge(x_done, TC * x_norm[u] + c + 1)
                    squares(u, c, x[:, c, :], out)
                    root(u, c)

            x_norm = {2: 0, 4: 1, 8: 2}
            warmed = [0]

            def warm(func):
                act.activation(warm_out[:, warmed[0]:warmed[0] + 1], ones[0:1, 0:1], func)
                warmed[0] += 1

            def modulated_hi(v):
                for b in range(4):
                    act.wait_ge(t_done, 4 * v + b + 1)
                    act.activation(hT_hi[:, 2 * b:2 * b + 2, :], t32[:, 2 * b:2 * b + 2, :], ACT.Copy)\
                        .then_inc(hThi, 1)

            def gain(n, w, b0):
                act.wait_ge(gate_mm, n + 1)
                act.activation(gate[w][:, :].rearrange("p (a b) -> p a b", a=2), ps[:, b0:b0 + 2, :],
                               ACT.Copy).then_inc(gain_ok, 1)

            def head_hi(g, n):
                act.wait_ge(pv_mm, n + 1)
                act.activation(hT_hi[:, 4 * g:4 * g + 4, :], ps[:, 4 * g:4 * g + 4, 0:T], ACT.Copy).then_inc(oT_hi, 1)

            act.wait_ge(consts, 1)
            warm(ACT.Silu)
            act.wait_ge(cols_ok, 1)
            act.activation(cond[:, :], cols[:, :, COND_ROW], ACT.Silu).then_inc(cond_ok, 1)
            warm(ACT.Sqrt)
            act.wait_ge(s_x, 16)
            for c in range(TC):
                squares(0, c, x[:, c, :])
            for c in range(TC):
                root(0, c)
            hi(0)
            hi(1)
            modulated_hi(0)

            def stick_hi(g):
                act.wait_ge(z_mm, 2 - g)
                link(act.activation(stick[g][:, :, :, :].rearrange("p h b n -> p h (b n)"),
                                    ps[:, 4 * g:4 * g + 4, 0:3 * P], ACT.Abs))
                link(act.activation(stick[g][:, :, :, :], stick[g][:, :, :, :], ACT.Exp, scale=-1.0))
                act.activation(stick[g][:, :, :, :], stick[g][:, :, :, :], ACT.Ln, bias=1.0).then_inc(ln_ok, 1)

            def stick_exp(g):
                act.wait_ge(tail_mm, 2 - g)
                act.activation(stick[g][:, :, :, :], ps[:, 4 * g:4 * g + 4, 0:3 * P].rearrange(
                    "p h (b n) -> p h b n", b=3), ACT.Exp).then_inc(a_ok, 1)

            for g in range(6):
                if g < 5:
                    hi(2 * g + 2)
                    hi(2 * g + 3)
                act.wait_ge(used, 2 * g + 2)
                for b in range(2):
                    if g < 4:
                        s, h = g // 2, 4 * (g % 2) + 2 * b
                        act.activation(qkT[:, h:h + 2, s * T:(s + 1) * T],
                                       ps[:, 2 * g + b, :].rearrange("p (a t) -> p a t", a=2), ACT.Copy,
                                       scale=(float(P) ** -0.5 if s == 0 else 1.0)).then_inc(ev_qkv, 1)
                    else:
                        act.activation(v0[:, b, (g - 4) * 512:(g - 3) * 512], ps[:, 2 * (g - 4) + b, :], ACT.Copy)\
                            .then_inc(ev_qkv, 1)
                if g == 1:
                    act.wait_ge(trig_a, 1)
                    act.activation(trig[:, :, :, :], ang[:, :, :, :], ACT.Sin).then_inc(trig_ok, 1)
                if g == 4:
                    stick_hi(1)
            M = first["sb_out"]
            hi(M)
            hi(M + 1)
            stick_exp(1)
            stick_hi(0)
            head_hi(1, 0)
            stick_exp(0)
            hi(M + 2)
            head_hi(0, 1)
            hi(M + 3)
            hi(M + 4)
            warm(ACT.Sqrt)
            gain(0, 0, 2)
            branch_squares(2, 1, 4, M + 3)
            hi(M + 5)
            modulated_hi(1)
            gain(1, 1, 6)
            M = first["gu"]

            def g_hi(j):
                act.wait_ge(hid_ok, j + 1)
                act.activation(gT_hi[:, 2 * j:2 * j + 2, :], hid[j % 2][:, :, :], ACT.Copy).then_inc(gThi, 1)

            for j in range(FG):
                hi(M + 2 * j + 2)
                if j >= 1:
                    g_hi(j - 1)
                hi(M + 2 * j + 3)
                act.wait_ge(used, M + 2 * j + 2)
                if j >= 2:
                    act.wait_ge(gTlo, j - 1)
                act.activation(hid[j % 2][:, :, :], ps[:, 2 * (j % 2), :].rearrange("p (a t) -> p a t", a=2), ACT.Silu)\
                    .then_inc(sil_ok, 1)
            M = first["down"]
            hi(M + 2)
            g_hi(FG - 1)
            for d in range(3, FG):
                hi(M + d)
            hi(M + FG)
            warm(ACT.Sqrt)
            branch_squares(4, 3, 0, M + FG - 1)
            M = first["mla_in"]
            hi(M + 1)
            modulated_hi(2)
            hi(M + 2)
            hi(M + 3)
            act.wait_ge(used, M + 2)
            for c in range(TC):
                squares(5, c, ps[:, c, 0:QL])
            for c in range(TC):
                squares(6, c, ps[:, c, QL:QL + KVL])
            for u in (5, 6):
                for c in range(TC):
                    root(u, c)
            gain(2, 0, 6)
            act.wait_ge(cT_ok, 1)
            act.activation(cT_hi[:, :, :], cT[:, :, :], ACT.Copy).then_inc(cThi, 1)
            hi(M + 4)
            for u in range(2):
                act.wait_ge(used, M + 3 + u)
                for c in range(TC):
                    for s in range(2):
                        act.activation(qn[:, c, u * 768 + s * 384:u * 768 + (s + 1) * 384],
                                       ps[:, 4 * (1 - u) + 2 * c + s, 0:384], ACT.Copy,
                                       scale=float(QW) ** -0.5).then_inc(ev_q, 1)
            act.wait_ge(used, M + 5)
            for c in (1, 0):
                for s in range(4):
                    act.activation(kvn[:, c, s * 512:(s + 1) * 512], ps[:, 4 * c + s, :], ACT.Copy).then_inc(ev_kv, 1)
            act.wait_ge(qT_mm, 1)
            act.activation(qnT[:, :, :].rearrange("p (b a) t -> p b (a t)", b=4), ps[:, 4:8, :], ACT.Copy)\
                .then_inc(qT_ok, 1)
            act.wait_ge(rT_mm, 1)
            act.activation(qrT[:, :, :].rearrange("p (b a) t -> p b (a t)", b=4), ps[0:ROPE, 4:8, :], ACT.Copy)\
                .then_inc(rT_a, 1)
            M = first["mla_out"]
            hi(M)
            hi(M + 1)
            for g in range(2):
                act.wait_ge(smax_ok, g + 1)
                for h in range(4):
                    act.activation(prob[g][:, h, 0, :], prob[g][:, h, 0, :], ACT.Exp, bias=nmax[:, g, 0, h:h + 1],
                                   accum_out=psum_p[:, g, 0, h:h + 1]).then_inc(exp_ok, 1)
                    act.activation(prob[g][:, h, 1:3, :], prob[g][:, h, 1:3, :], ACT.Exp, bias=nmax[:, g, 1, h:h + 1],
                                   accum_out=psum_p[:, g, 1, h:h + 1]).then_inc(exp_ok, 1)
            for g in range(2):
                head_hi(g, 2 + g)
            for k in range(2, 4):
                hi(M + k)
            warm(ACT.Sqrt)
            branch_squares(8, 7, 0, M + 3, mjunk)
            modulated_hi(3)
            act.activation(wr_hi[:, :, :], wr[:, :, :], ACT.Copy).then_inc(wr_cut, 1)
            warm(ACT.Exp)

            act.wait_ge(lg_mm, 1)
            act.activation(xhat_hi[:, :, :], xhat[:, :, :], ACT.Copy).then_inc(xs_hi, 1)
            act.wait_ge(wt_a, 1)
            act.activation(wt[:, 1, :], diff[:, :], ACT.Exp).then_inc(wt_ok, 1)
            gain(3, 1, 6)

            def x_out(n):
                for b in range(2):
                    act.wait_ge(e_gath, n + b + 1)
                    for a in range(4):
                        k = 4 * b + a
                        ins = act.activation(xe32[:, k, :], ps[:, b, a * P:(a + 1) * P], ACT.Identity,
                                             scale=scale[:, 3, k:k + 1], bias=shift[:, 3, k:k + 1])
                    ins.then_inc(e_t, 1)
                for b in range(2):
                    act.wait_ge(e_t, n + b + 1)
                    act.activation(xe_hi[:, 4 * b:4 * b + 4, :], xe32[:, 4 * b:4 * b + 4, :], ACT.Copy)\
                        .then_inc(e_xhi, 1)

            def y_out(n):
                act.wait_ge(used, n)
                act.activation(ye_hi[:, :].rearrange("p (a b) -> p a b", a=2), ps[:, 4:6, :], ACT.Copy)\
                    .then_inc(e_y, 1)

            x_out(0)
            act.wait_ge(visit_ok, 1)
            last = act.value_load(n_end[0:1, 0:1], min_val=E, max_val=2 * E)
            act.wait_ge(e_blank, 1)
            with act.Fori(0, last) as i:
                def ehi(k):
                    wait_expert_piece(act, i, k)
                    act.wait_ge(used, M0 + k - NB + 1 + NK * i)
                    n_c = piece_elems(expert_piece(0, k)[1])
                    act.activation(m_hi[k % NB][:, 0:n_c], ring[(N0 + k) % R][:, 0:n_c], ACT.Copy)\
                        .then_inc(hi_done, 1)

                def eg_hi(j):
                    act.wait_ge(e_hidT, EG * i + j + 1)
                    n_f = gw[j] // P
                    act.activation(eT_hi[:, 2 * j:2 * j + n_f, :].rearrange("p a b -> p (a b)"),
                                   ps[:, 2 + j % 2, 0:gw[j]], ACT.Copy).then_inc(e_ghi, 1)

                ehi(0)
                ehi(1)
                ehi(2)
                y_out(M0 + NK * i)
                for j in range(EG):
                    ehi(2 * j + 3)
                    if j >= 1:
                        eg_hi(j - 1)
                    act.wait_ge(used, M0 + 2 * j + 2 + NK * i)
                    if j >= 2:
                        act.wait_ge(e_hid, EG * i + j - 1)
                    act.activation(esil[j % 2][:, 0:gw[j]], ps[:, j % 2, 0:gw[j]], ACT.Silu).then_inc(e_sil, 1)
                    if j == 4:
                        act.wait_ge(e_pT, i + 1)
                        act.activation(spread[:, :], ps[:, 6, 0:T], ACT.Copy)
                    ehi(2 * j + 4)
                ehi(2 * EG + 3)
                eg_hi(EG - 1)
                ehi(2 * EG + 4)
                x_out(2 * i + 2)
                ehi(2 * EG + 5)
            y_out(M0 + NK * last)
            warm(ACT.Sqrt)
            for c in range(TC):
                act.wait_ge(e_add, 2 * last + 1 + c)
                squares(9, c, macc[:, c, :], mjunk)
                root(9, c)
            for c in range(TC):
                act.wait_ge(x_done, 3 * TC + c + 1)
                act.dma_start(out_d[0, c * P:(c + 1) * P, :], x[:, c, :]).then_inc(s_out, 16)
            act.wait_ge(s_out, 32)

        @block.vector
        def _(dve):
            link = chain(dve, dve_step)
            pieces = [0]

            def lo(m):
                n = no_of[m]
                assert n == pieces[0], (n, pieces)
                pieces[0] += 1
                dve.wait_ge(hi_done, m + 1)
                cols_n = piece_elems(stream[n][3])
                dve.tensor_tensor(w_lo[m % 2][:, 0:cols_n], ring[n % R][:, 0:cols_n],
                                  w_hi[m % 2][:, 0:cols_n].bitcast(F32), ALU.subtract).then_inc(freed, 1)

            def ada(count):
                for _ in range(count):
                    n = pieces[0]
                    assert stream[n][0] == "ada"
                    pieces[0] += 1
                    _, third, k = stream[n][1]
                    dst = acc[:, third * 2048:third * 2048 + 2048]
                    wait_piece(dve, n)
                    if k == 0:
                        dve.tensor_scalar(dst, ring[n % R][:, :], cond[:, 0:1], None, ALU.mult).then_inc(freed, 1)
                    else:
                        dve.wait_ge(freed, n)
                        dve.scalar_tensor_tensor(dst, ring[n % R][:, :], cond[:, k:k + 1], dst, ALU.mult,
                                                 ALU.add).then_inc(freed, 1)

            def mean_square(u, c, width):
                dve.wait_ge(ss_done, TC * u + c + 1)
                dve.tensor_scalar(ssq[:, u, c:c + 1], ssq[:, u, c:c + 1], 1.0 / width, EPS, ALU.mult, ALU.add)\
                    .then_inc(var_done, 1)

            def inverse_root(u, c, width):
                dve.wait_ge(root_done, TC * u + c + 1)
                dve.reciprocal(rstd[:, u, c:c + 1], rstd[:, u, c:c + 1]).then_inc(rstd_done, 1)

            def rms(u, c, width):
                mean_square(u, c, width)
                inverse_root(u, c, width)
                dve.wait_ge(rstd_done, TC * u + c + 1)

            def normalise(u):
                for c in range(TC):
                    rms(u, c, D)
                    dve.tensor_scalar(xhat[:, c, :], x[:, c, :], rstd[:, u, c:c + 1], None, ALU.mult)\
                        .then_inc(xhat_done, 1)

            def modulated(v, between=()):
                def cut(b):
                    dve.wait_ge(hThi, 4 * v + b + 1)
                    dve.tensor_tensor(hT_lo[:, 2 * b:2 * b + 2, :], t32[:, 2 * b:2 * b + 2, :],
                                      hT_hi[:, 2 * b:2 * b + 2, :].bitcast(F32), ALU.subtract).then_inc(hTlo, 1)

                for b in range(4):
                    dve.wait_ge(tr_done, 4 * v + b + 1)
                    for a in range(2):
                        k = 2 * b + a
                        ins = dve.tensor_scalar(t32[:, k, :], ps[:, b, a * T:(a + 1) * T], scale[:, v, k:k + 1],
                                                shift[:, v, k:k + 1], ALU.mult, ALU.add)
                    ins.then_inc(t_done, 1)
                    if b:
                        cut(b - 1)
                cut(3)

            def mod_cols(v, b):
                l, w = divmod(v, 2)
                dve.wait_ge(mod_mm, v + 1)
                dve.tensor_tensor(shift[:, v, :], ps[:, b, 0:DC], cols[:, :, 6 * l + 3 * w], ALU.add)
                link(dve.tensor_tensor(scale[:, v, :], ps[:, b, DC:2 * DC], cols[:, :, 6 * l + 3 * w + 1], ALU.add))
                dve.scalar_tensor_tensor(scale[:, v, :], scale[:, v, :], 1.0, cols[:, :, 12 + 4 * l + 2 * w],
                                         ALU.add, ALU.mult).then_inc(mod_ok, 1)
                dve.wait_ge(mod_ok, v + 1)

            def gate_rows(n, w, b0):
                dve.wait_ge(gain_ok, n + 1)
                dve.wait_ge(gate_mm, n + 1)
                g = gate[w][:, :].rearrange("p (a b) -> p a b", a=2)
                dve.tensor_tensor(g, ps[:, b0:b0 + 2, :], g, ALU.mult).then_inc(gate_ok, 1)

            def residual(q, u, srcs, w):
                for c in range(TC):
                    rms(u, c, D)
                    dst, g = xhat[:, c, :], gate[w][:, :]
                    if len(srcs[c].shape) == 3:
                        dst, g = (a.rearrange("p (a b) -> p a b", a=2) for a in (dst, g))
                    link(dve.scalar_tensor_tensor(dst, srcs[c], rstd[:, u, c:c + 1], g, ALU.mult, ALU.mult))
                    dve.tensor_tensor(x[:, c, :], x[:, c, :], xhat[:, c, :], ALU.add).then_inc(x_done, 1)
                dve.wait_ge(x_done, TC * (q + 1))

            def head_lo(g, n):
                dve.wait_ge(oT_hi, n + 1)
                dve.tensor_tensor(hT_lo[:, 4 * g:4 * g + 4, :], ps[:, 4 * g:4 * g + 4, 0:T],
                                  hT_hi[:, 4 * g:4 * g + 4, :].bitcast(F32), ALU.subtract).then_inc(oT_lo, 1)

            dve.wait_ge(rowsT, 1)
            dve.tensor_copy(cols[:, :, :], ps[:, 5, 0:DC * NROWS].rearrange("p (k r) -> p k r", k=DC)).then_inc(cols_ok, 1)
            dve.wait_ge(s_x, 16)
            dve.wait_ge(cond_ok, 1)
            normalise(0)
            ada(DC)
            mod_cols(0, 4)
            lo(0)
            ada(1)
            modulated(0)
            lo(1)
            ada(1)
            lo(2)
            dve.wait_ge(freqT, 1)
            dve.tensor_copy(lat_g[:, :], ps[:, 6, HR:HR + 3])
            dve.tensor_copy(ident_r[:, :], ident[:, :])
            dve.wait_ge(s_small, 48)
            link(dve.tensor_copy(pos_f[:, :], pos_i[:, :]))
            for c in range(TC):
                for s in range(2):
                    ins = dve.tensor_scalar(ang[:, s, c, :], ps[:, 6, 0:HR], pos_f[:, c:c + 1], None, ALU.mult)
            ins.then_inc(freq_ok, 1)
            dve.wait_ge(freq_ok, 1)
            for s, quarter in ((0, 0.25), (1, 0.0)):
                ins = dve.tensor_scalar(turns[:, s, :, :], ang[:, s, :, :], 1.0 / TWO_PI, quarter, ALU.mult, ALU.add)
            link(ins)
            link(dve.tensor_scalar(turns[:, :, :, :], turns[:, :, :, :], MAGIC, MAGIC, ALU.add, ALU.subtract))
            for part in (PI_A, PI_B, PI_C):
                flat = [a[:, :, :, :].rearrange("p s c f -> p (s c f)") for a in (ang, turns)]
                link(dve.scalar_tensor_tensor(flat[0], flat[1], -part, flat[0], ALU.mult, ALU.add))
            link(dve.tensor_scalar(ang[:, 0, :, :], ang[:, 0, :, :], TWO_PI / 4, None, ALU.add))
            dve.tensor_scalar(ang[:, :, :, :], ang[:, :, :, :], PI_MAX, -PI_MAX, ALU.min, ALU.max).then_inc(trig_a, 1)
            ada(1)

            def softplus(g):
                dve.wait_ge(ln_ok, 2 - g)
                flat = stick[g][:, :, :, :].rearrange("p h b n -> p h (b n)")
                dve.scalar_tensor_tensor(flat, ps[:, 4 * g:4 * g + 4, 0:3 * P], 0.0, flat, ALU.max, ALU.add)\
                    .then_inc(sp_ok, 1)

            for m in range(3, 12):
                lo(m)
                if m < 10:
                    ada(1)
            M = first["sb_out"]
            softplus(1)
            lo(M)
            lo(M + 1)
            ada(1)
            softplus(0)
            head_lo(1, 0)
            ada(3)
            lo(M + 2)
            ada(1)
            head_lo(0, 1)
            lo(M + 3)
            ada(1)
            lo(M + 4)
            gate_rows(0, 0, 0)
            residual(0, 1, [ps[:, 4:6, :], ps[:, 6:8, :]], 0)
            mod_cols(1, 0)
            normalise(2)
            modulated(1)
            lo(M + 5)
            ada(2)
            gate_rows(1, 1, 4)
            M = first["gu"]

            def g_lo(j):
                dve.wait_ge(gThi, j + 1)
                dve.tensor_tensor(gT_lo[:, 2 * j:2 * j + 2, :], hid[j % 2][:, :, :],
                                  gT_hi[:, 2 * j:2 * j + 2, :].bitcast(F32), ALU.subtract).then_inc(gTlo, 1)

            for j in range(FG):
                lo(M + 2 * j + 2)
                if j >= 1:
                    g_lo(j - 1)
                if j + 1 == FG:
                    ada(1)
                lo(M + 2 * j + 3)
                dve.wait_ge(sil_ok, j + 1)
                dve.tensor_tensor(hid[j % 2][:, :, :], hid[j % 2][:, :, :],
                                  ps[:, 2 * (j % 2) + 1, :].rearrange("p (a t) -> p a t", a=2), ALU.mult)\
                    .then_inc(hid_ok, 1)
                if j + 1 < FG:
                    ada(2 if j == 0 else 1)
            M = first["down"]
            ada(1)
            lo(M + 2)
            g_lo(FG - 1)
            ada(1)
            for d in range(3, FG):
                lo(M + d)
                ada(1)
            M = first["mla_in"]
            lo(M)
            residual(1, 3, [ps[:, 0:2, :], ps[:, 2:4, :]], 1)
            normalise(4)
            mod_cols(2, 4)
            modulated(2)
            lo(M + 1)
            lo(M + 2)
            latents = [(u, c, width) for u, width in ((5, QL), (6, KVL)) for c in range(TC)]
            for part in (mean_square, inverse_root):
                for u, c, width in latents:
                    part(u, c, width)
            dve.wait_ge(rstd_done, TC * 7)
            for c in range(TC):
                dve.tensor_scalar(lat[:, c, 0:QL], ps[:, c, 0:QL], rstd[:, 5, c:c + 1], None, ALU.mult)
                dve.tensor_scalar(lat[:, c, QL:QL + KVL], ps[:, c, QL:QL + KVL], rstd[:, 6, c:c + 1], None, ALU.mult)
                ins = dve.tensor_copy(kr[:, c, :], ps[:, c, QL + KVL:MLA_IN])
            ins.then_inc(lat_ok, 1)
            gate_rows(2, 0, 4)
            lo(M + 3)
            dve.wait_ge(lat_T, 1)
            for k in range(3):
                ins = dve.tensor_scalar(cT[:, k, :], ps[:, 2 + k // 2, (k % 2) * T:(k % 2 + 1) * T], lat_g[:, k:k + 1],
                                        None, ALU.mult)
            ins.then_inc(cT_ok, 1)
            dve.wait_ge(cThi, 1)
            dve.tensor_tensor(cT_lo[:, :, :], cT[:, :, :], cT_hi[:, :, :].bitcast(F32), ALU.subtract).then_inc(cTlo, 1)
            lo(M + 4)
            dve.wait_ge(trig_ok, 1)
            dve.wait_ge(lat_ok, 1)

            def rotate(x1, x2, cos, sin, t):
                dve.tensor_tensor(t[0], x1, cos, ALU.mult)
                dve.tensor_tensor(t[1], x2, sin, ALU.mult)
                dve.tensor_tensor(t[2], x2, cos, ALU.mult)
                link(dve.tensor_tensor(t[3], x1, sin, ALU.mult))
                dve.tensor_tensor(x1, t[0], t[1], ALU.subtract)
                return dve.tensor_tensor(x2, t[2], t[3], ALU.add)

            for c in range(TC):
                link(rotate(kr[:, c, 0:HR], kr[:, c, HR:ROPE], trig[:, 0, c, :], trig[:, 1, c, :],
                            [rt[:, n, 0, :] for n in range(4)]))
            dve.wait_ge(ev_q, 8)
            for c in range(TC):
                q = qn[:, c, :].rearrange("p (h w) -> p h w", h=MLA_H)
                cos, sin = (trig[:, s, c, :].unsqueeze(1).broadcast_to([P, MLA_H, HR]) for s in range(2))
                ins = rotate(q[:, :, NOPE:NOPE + HR], q[:, :, NOPE + HR:QW], cos, sin, [rt[:, n, :, :] for n in range(4)])
                if c + 1 < TC:
                    link(ins)
            ins.then_inc(rope_ok, 1)
            dve.wait_ge(kT_mm, 1)
            dve.tensor_copy(knT[:, :, :].rearrange("p (b a) t -> p b (a t)", b=4), ps[:, 0:4, :]).then_inc(kT_ok, 1)
            dve.wait_ge(rT_mm, 2)
            dve.tensor_copy(krT[:, :], ps[0:ROPE, 0, 0:T]).then_inc(rT_d, 1)
            M = first["mla_out"]
            lo(M)
            lo(M + 1)
            for g in range(2):
                dve.wait_ge(s_mm, g + 1)
                sc = ps[:, 4 * g:4 * g + 4, 0:3 * P].rearrange("p h (b n) -> p h b n", b=3)
                dve.tensor_copy(prob[g][:, :, 1, :], sc[:, :, 1, :])
                link(dve.tensor_tensor(prob[g][:, :, 0, :], sc[:, :, 0, :],
                                       causal[:, :].unsqueeze(1).broadcast_to([P, 4, P]), ALU.add))
                link(dve.tensor_tensor(prob[g][:, :, 2, :], sc[:, :, 2, :],
                                       causal[:, :].unsqueeze(1).broadcast_to([P, 4, P]), ALU.add))
                dve.tensor_reduce(nmax[:, g, 0, :], prob[g][:, :, 0, :], AX.X, ALU.max, negate=True)
                dve.tensor_reduce(nmax[:, g, 1, :], prob[g][:, :, 1:3, :].rearrange("p h b n -> p h (b n)"), AX.X,
                                  ALU.max, negate=True).then_inc(smax_ok, 1)
            for g in range(2):
                dve.wait_ge(exp_ok, 8 * (g + 1))
                link(dve.reciprocal(rsum[:, g, :, :], psum_p[:, g, :, :]))
                dve.tensor_tensor(prob[g][:, :, 0, :], prob[g][:, :, 0, :],
                                  rsum[:, g, 0, :].unsqueeze(2).broadcast_to([P, 4, P]), ALU.mult)
                late = prob[g][:, :, 1:3, :].rearrange("p h b n -> p h (b n)")
                dve.tensor_tensor(late, late, rsum[:, g, 1, :].unsqueeze(2).broadcast_to([P, 4, 2 * P]),
                                  ALU.mult).then_inc(prob_ok, 1)
            for g in range(2):
                dve.wait_ge(pT_mm, g + 1)
                dve.tensor_copy(prob[g][:, :, :, :].rearrange("p h b n -> p h (b n)"),
                                ps[:, 4 * g:4 * g + 4, 0:3 * P]).then_inc(pT_ok, 1)
            for g in range(2):
                head_lo(g, 2 + g)
            dve.memset(macc[:, :, :], 0.0)
            dve.memset(spread[:, :].bitcast(F32), 0.0)
            lo(M + 2)
            lo(M + 3)
            residual(2, 7, [ps[:, 0:2, :], ps[:, 2:4, :]], 0)
            normalise(8)
            mod_cols(3, 4)
            modulated(3)
            dve.wait_ge(wr_cut, 1)
            dve.tensor_tensor(wr_lo[:, :, :], wr[:, :, :], wr_hi[:, :, :].bitcast(F32), ALU.subtract).then_inc(wr_cut, 1)
            dve.memset(visit[:, :, :], 0.0).then_inc(visit_0, 1)
            dve.wait_ge(lgT_mm, 1)
            dve.tensor_scalar(lgT[:, :], ps[0:E, 3, 0:T], br[:, 0:1], None, ALU.add).then_inc(lgT_ok, 1)
            dve.wait_ge(lg_mm, 1)
            link(dve.tensor_copy(lg[:, :, :], ps[:, 3, 0:TC * E].rearrange("p (c e) -> p c e", c=TC)))

            def best(logits, top, one):
                def both(step):
                    step(0)
                    link(step(1))
                both(lambda c: dve.max(top[:, c, :], logits[:, c, :]))
                both(lambda c: dve.scalar_tensor_tensor(eq[:, c, :], logits[:, c, :], top[:, c, 0:1], eight[:, :],
                                                        ALU.is_equal, ALU.mult))
                both(lambda c: dve.max(kmax[:, c, :], eq[:, c, :]))
                both(lambda c: dve.tensor_scalar(one[:, c, :], eq[:, c, :], kmax[:, c, 0:1], None, ALU.is_equal))

            best(lg, top8, one1)
            link(dve.scalar_tensor_tensor(lg2[:, :, :].rearrange("p c e -> p (c e)"),
                                          one1[:, :, :].rearrange("p c e -> p (c e)"), NEG,
                                          lg[:, :, :].rearrange("p c e -> p (c e)"), ALU.mult, ALU.add))
            best(lg2, top8b, one2)
            dve.tensor_tensor(member[:, :, :], one1[:, :, :], one2[:, :, :], ALU.add).then_inc(member_ok, 1)
            dve.tensor_tensor(diff[:, :], top8b[:, :, 0], top8[:, :, 0], ALU.subtract).then_inc(wt_a, 1)
            dve.wait_ge(xs_hi, 1)
            dve.tensor_tensor(xhat_lo[:, :, :], xhat[:, :, :], xhat_hi[:, :, :].bitcast(F32), ALU.subtract)\
                .then_inc(xs_lo, 1)
            dve.wait_ge(wt_ok, 1)
            link(dve.tensor_scalar(wt[:, 0, :], wt[:, 1, :], 1.0, None, ALU.add))
            link(dve.reciprocal(wt[:, 0, :], wt[:, 0, :]))
            link(dve.tensor_tensor(wt[:, 1, :], wt[:, 1, :], wt[:, 0, :], ALU.mult))
            dve.wait_ge(visit_0, 1)
            dve.wait_ge(pos_mm, 1)
            dve.wait_ge(member_ok, 1)
            for c in range(TC):
                where = ps[:, 3, 32 + c * E:32 + (c + 1) * E]
                dve.tensor_copy(visit[:, 0:E, 3 * c], where)
                dve.tensor_scalar(visit[:, E:2 * E, 3 * c], where, float(-CAP), None, ALU.add)
                link(dve.tensor_scalar(one1[:, c, :], one1[:, c, :], wt[:, 0, c:c + 1], None, ALU.mult))
                for r in range(2):
                    dve.tensor_copy(visit[:, E * r:E * (r + 1), 3 * c + 1], member[:, c, :])
                    ins = dve.scalar_tensor_tensor(visit[:, E * r + 1:E * (r + 1) + 1, 3 * c + 2], one2[:, c, :],
                                                   wt[:, 1, c:c + 1], one1[:, c, :], ALU.mult, ALU.add)
                link(ins)
            link(dve.tensor_reduce(count_f[:, :], ps[:, 3, 48:48 + E], AX.X, ALU.max))
            link(dve.tensor_scalar(count_f[:, :], count_f[:, :], float(CAP), float(E), ALU.is_gt, ALU.mult))
            dve.tensor_scalar(n_end[:, :], count_f[:, :], float(E), None, ALU.add).then_inc(visit_ok, 1)

            def picks(loop_link, i):
                loop_link(dve.tensor_copy(cur[:, :], visit[:, i, :]))
                for c in range(TC):
                    ins = dve.tensor_scalar(pick[:, c, :], slot_no[:, :], cur[:, 3 * c:3 * c + 1],
                                            cur[:, 3 * c + 1:3 * c + 2], ALU.is_equal, ALU.mult)
                ins.then_inc(e_pick, 1)

            def x_lo(n):
                for b in range(2):
                    dve.wait_ge(e_xhi, n + b + 1)
                    dve.tensor_tensor(xe_lo[:, 4 * b:4 * b + 4, :], xe32[:, 4 * b:4 * b + 4, :],
                                      xe_hi[:, 4 * b:4 * b + 4, :].bitcast(F32), ALU.subtract).then_inc(e_xlo, 1)

            def y_lo(n):
                dve.wait_ge(e_y, n)
                dve.tensor_tensor(ye_lo[:, :].rearrange("p (a b) -> p a b", a=2), ps[:, 4:6, :],
                                  ye_hi[:, :].bitcast(F32).rearrange("p (a b) -> p a b", a=2), ALU.subtract)\
                    .then_inc(e_ylo, 1)

            def collect(n, c, b0=6):
                dve.wait_ge(e_sc, n)
                m = macc[:, c, :].rearrange("p (a b) -> p a b", a=2)
                dve.scalar_tensor_tensor(m, ps[:, b0:b0 + 2, :], cur[:, 3 * c + 2:3 * c + 3], m, ALU.mult, ALU.add)\
                    .then_inc(e_add, 1)

            picks(link, 0)
            gate_rows(3, 1, 4)
            dve.wait_ge(gate_ok, 4)
            dve.memset(ps[:, 4:6, :], 0.0).then_inc(e_blank, 1)
            x_lo(0)
            last = dve.value_load(n_end[0:1, 0:1], min_val=E, max_val=2 * E)
            with dve.Fori(0, last) as i:
                def loop_link(ins):
                    ins.then_inc(e_step, 1)
                    dve.wait_ge(e_step, i + 1)

                def elo(k):
                    dve.wait_ge(hi_done, M0 + k + 1 + NK * i)
                    n_c = piece_elems(expert_piece(0, k)[1])
                    dve.tensor_tensor(m_lo[k % NB][:, 0:n_c], ring[(N0 + k) % R][:, 0:n_c],
                                      m_hi[k % NB][:, 0:n_c].bitcast(F32), ALU.subtract).then_inc(freed, 1)

                def eg_lo(j):
                    dve.wait_ge(e_ghi, EG * i + j + 1)
                    n_f = gw[j] // P
                    dve.tensor_tensor(eT_lo[:, 2 * j:2 * j + n_f, :].rearrange("p a b -> p (a b)"),
                                      ps[:, 2 + j % 2, 0:gw[j]],
                                      eT_hi[:, 2 * j:2 * j + n_f, :].bitcast(F32).rearrange("p a b -> p (a b)"),
                                      ALU.subtract).then_inc(e_glo, 1)

                elo(0)
                elo(1)
                elo(2)
                y_lo(i + 1)
                for j in range(EG):
                    elo(2 * j + 3)
                    if j >= 1:
                        eg_lo(j - 1)
                    dve.wait_ge(e_sil, EG * i + j + 1)
                    dve.tensor_tensor(ehid[j % 2][:, 0:gw[j]], esil[j % 2][:, 0:gw[j]],
                                      ps[:, j % 2, gw[j]:2 * gw[j]], ALU.mult).then_inc(e_hid, 1)
                    elo(2 * j + 4)
                    if j in (1, 2):
                        collect(2 * i + j, j - 1)
                    if j == 4:
                        dve.wait_ge(e_pT, i + 1)
                        picks(loop_link, i + 1)
                elo(2 * EG + 3)
                eg_lo(EG - 1)
                elo(2 * EG + 4)
                x_lo(2 * i + 2)
                elo(2 * EG + 5)
            y_lo(last + 1)
            collect(2 * last + 1, 0)
            collect(2 * last + 2, 1, 4)
            dve.wait_ge(e_add, 2 * last + 2)
            residual(3, 9, [macc[:, 0, :], macc[:, 1, :]], 1)
            assert pieces[0] == N0

        @block.tensor
        def _(pe):
            def three(out, a_hi, a_lo, b_hi, b_lo, start, stop):
                pe.matmul(out, a_hi, b_lo, start=start, stop=False)
                pe.matmul(out, a_hi, b_hi, start=False, stop=False)
                return pe.matmul(out, a_lo, b_hi, start=False, stop=stop)

            def product(m, k0, groups, a_hi, a_lo, begin, end, signal_c0=False):
                n = no_of[m]
                pe.wait_ge(freed, n + 1)
                shape = stream[n][3]
                kc, width = shape[0], piece_elems(shape[1:])
                bh = w_hi[m % 2][:, 0:kc * width].rearrange("p (k n) -> p k n", k=kc)
                bl = w_lo[m % 2][:, 0:kc * width].rearrange("p (k n) -> p k n", k=kc)
                for c in range(TC):
                    for c0, cn, out in groups:
                        for k in range(kc):
                            ins = three(out(c), a_hi[:, k0 + k, c * P:(c + 1) * P], a_lo[:, k0 + k, c * P:(c + 1) * P],
                                        bh[:, k, c0:c0 + cn], bl[:, k, c0:c0 + cn],
                                        begin and k == 0, end and k == kc - 1)
                    if signal_c0 and c == 0:
                        ins.then_inc(c0_done, 1)
                ins.then_inc(used, 1)

            def product_T(m, k0, b0, begin, end):
                pe.wait_ge(freed, no_of[m] + 1)
                bh = w_hi[m % 2][:, :].rearrange("p (k n) -> p k n", k=4)
                bl = w_lo[m % 2][:, :].rearrange("p (k n) -> p k n", k=4)
                for f in range(4):
                    o = ps[:, b0 + f // 2, (f % 2) * T:(f % 2 + 1) * T]
                    for k in range(4):
                        w_h, w_l = bh[:, k, f * P:(f + 1) * P], bl[:, k, f * P:(f + 1) * P]
                        pe.matmul(o, w_h, hT_lo[:, k0 + k, :], start=(begin and k == 0 and f % 2 == 0), stop=False,
                                  skip_group_check=True)
                        pe.matmul(o, w_h, hT_hi[:, k0 + k, :], start=False, stop=False, skip_group_check=True)
                        ins = pe.matmul(o, w_l, hT_hi[:, k0 + k, :], start=False,
                                        stop=(end and k == 3 and f % 2 == 1), skip_group_check=True)
                ins.then_inc(used, 1)

            def transpose_xhat(v):
                for c in range(TC):
                    pe.wait_ge(xhat_done, TC * v + c + 1)
                    for b in range(4):
                        for a in range(2):
                            k = 2 * b + a
                            ins = pe.transpose(ps[:, b, a * T + c * P:a * T + (c + 1) * P],
                                               xhat[:, c, k * P:(k + 1) * P], ident[:, :])
                        if c + 1 == TC:
                            ins.then_inc(tr_done, 1)

            def mod_columns(v, b):
                l, w = divmod(v, 2)
                for s in range(2):
                    for k in range(DC):
                        ins = pe.matmul(ps[:, b, s * DC + k:s * DC + k + 1],
                                        acc[:, (3 * w + s) * D + k * P:(3 * w + s) * D + (k + 1) * P],
                                        ones[:, 0:1], start=True, stop=True)
                ins.then_inc(mod_mm, 1)

            def gate_spread(l, w, b0):
                s = 3 * w + 2
                for a in range(2):
                    pe.matmul(ps[:, b0 + a, :], ones[:, :], acc[:, s * D + a * 512:s * D + (a + 1) * 512],
                              start=True, stop=False)
                    pe.matmul(ps[:, b0 + a, :], ident[0:NROWS, 6 * l + s:6 * l + s + 1].to_broadcast([NROWS, P]),
                              rows[0:NROWS, a * 512:(a + 1) * 512], start=False, stop=True)
                for a in range(2):
                    r = 12 + 4 * l + 2 * w + 1
                    ins = pe.matmul(ps[:, b0 + 2 + a, :], ident[0:NROWS, r:r + 1].to_broadcast([NROWS, P]),
                                    rows[0:NROWS, a * 512:(a + 1) * 512], start=True, stop=True)
                ins.then_inc(gate_mm, 1)

            def ada_ready(l, thirds):
                pe.wait_ge(freed, ada_no[(l, thirds, DC - 1)] + 1)

            def bank(base_, step):
                return lambda c: ps[:, base_ + step * c, :]

            pe.wait_ge(idn, 1)
            pe.wait_ge(consts, 9)
            pe.wait_ge(s_rows, 16 * 3)
            for k in range(DC):
                ins = pe.transpose(ps[:, 5, k * NROWS:(k + 1) * NROWS], rows[0:NROWS, k * P:(k + 1) * P],
                                   ident[0:NROWS, 0:NROWS])
            ins.then_inc(rowsT, 1)
            transpose_xhat(0)

            def keep_clock(n):
                for _ in range(n):
                    pe.matmul(ps[:, 7, 0:P], ones[:, :], ones[:, :], start=True, stop=True)

            pe.wait_ge(freed, 6)
            keep_clock(8)
            ada_ready(0, 0)
            mod_columns(0, 4)
            keep_clock(20)
            for g in range(4):
                for h in range(2):
                    if g == 0:
                        pe.wait_ge(hTlo, 2 * h + 2)
                    if g == 2:
                        pe.wait_ge(mod_ok, 1)
                    product_T(2 * g + h, 4 * h, 2 * g, h == 0, h == 1)
                if g == 0:
                    pe.wait_ge(s_lat, 48)
                    pe.matmul(ps[:, 6, 0:HR], ones[0:1, :], freq[0:1, :], start=True, stop=True)
                    pe.transpose(ps[:, 6, HR:HR + 3], lat_rows[0:3, :], ident[0:3, 0:3]).then_inc(freqT, 1)
                if g == 2:
                    pe.wait_ge(freq_ok, 1)

            def scores_T(g):
                for h in range(4 * g, 4 * g + 4):
                    pe.matmul(ps[:, h, 0:T], qkT[:, h, T:T + P], qkT[:, h, 0:T], start=True, stop=False,
                              skip_group_check=True)
                    ins = pe.matmul(ps[:, h, T:T + P], qkT[:, h, T + P:2 * T], qkT[:, h, P:T], start=False,
                                    stop=False, skip_group_check=True)
                ins.then_inc(z_mm, 1)

            def tails(g):
                pe.wait_ge(sp_masked, 2 * (2 - g))
                for h in range(4):
                    o, s = ps[:, 4 * g + h, :], stick[g][:, h, :, :].rearrange("p b n -> p (b n)")
                    pe.matmul(o[:, 0:T], neg_ge[:, :], s[:, 0:T], start=False, stop=False, skip_group_check=True)
                    pe.matmul(o[:, P:T], neg_one[:, :], s[:, T:T + P], start=False, stop=False, skip_group_check=True)
                    ins = pe.matmul(o[:, T:T + P], neg_ge[:, :], s[:, T:T + P], start=False, stop=True,
                                    skip_group_check=True)
                ins.then_inc(tail_mm, 1)

            def weighted_values(g, p, value):
                for h in range(4):
                    o, s = ps[:, 4 * g + h, :], p[g][:, h, :, :].rearrange("p b n -> p (b n)")
                    pe.matmul(o[:, 0:T], value(0, 4 * g + h), s[:, 0:T], start=True, stop=False, skip_group_check=True)
                    ins = pe.matmul(o[:, P:T], value(1, 4 * g + h), s[:, T:T + P], start=False, stop=True,
                                    skip_group_check=True)
                ins.then_inc(pv_mm, 1)

            def value0(c, h):
                return v0[:, c, h * P:(h + 1) * P]

            for g in (4, 5):
                pe.wait_ge(ev_qkv, 2 * (g - 3))
                for h in range(2):
                    product(2 * g + h, 4 * h, [(0, 512, bank(2 * (g - 4), 1))], hT_hi, hT_lo, h == 0, h == 1)
                if g == 4:
                    pe.wait_ge(ev_qkv, 8)
                    scores_T(1)
            tails(1)
            pe.wait_ge(ev_qkv, 12)
            scores_T(0)
            pe.wait_ge(a_masked, 2)
            weighted_values(1, stick, value0)
            M = first["sb_out"]
            tails(0)
            pe.wait_ge(oT_lo, 1)
            product(M, 4, [(0, 512, bank(4, 2))], hT_hi, hT_lo, True, False)
            product(M + 1, 4, [(0, 512, bank(5, 2))], hT_hi, hT_lo, True, False)
            pe.wait_ge(a_masked, 4)
            weighted_values(0, stick, value0)
            pe.wait_ge(oT_lo, 2)
            product(M + 2, 0, [(0, 512, bank(4, 2))], hT_hi, hT_lo, False, True)
            ada_ready(0, 1)
            gate_spread(0, 0, 0)
            product(M + 3, 0, [(0, 512, bank(5, 2))], hT_hi, hT_lo, False, True, True)
            ada_ready(0, 2)
            pe.wait_ge(gate_ok, 1)
            mod_columns(1, 0)
            pe.wait_ge(mod_ok, 2)
            transpose_xhat(1)
            gate_spread(0, 1, 4)
            M = first["gu"]
            for j in range(FG):
                if j >= 2:
                    pe.wait_ge(hid_ok, j - 1)
                for h in range(2):
                    if j == 0:
                        pe.wait_ge(hTlo, 6 + 2 * h)
                    product_T(M + 2 * j + h, 4 * h, 2 * (j % 2), h == 0, h == 1)
            M = first["down"]
            pe.wait_ge(hid_ok, FG)
            halves = [(0, 512, bank(0, 2)), (512, 512, bank(1, 2))]
            for d in range(FG):
                pe.wait_ge(gTlo, d + 1)
                product(M + d, 2 * d, halves, gT_hi, gT_lo, d == 0, d == FG - 1, d == FG - 1)
            ada_ready(1, 2)
            pe.wait_ge(gate_ok, 2)
            mod_columns(2, 4)
            transpose_xhat(2)
            M = first["mla_in"]
            for h in range(2):
                pe.wait_ge(hTlo, 10 + 2 * h)
                product(M + h, 4 * h, [(0, MLA_IN, lambda c: ps[:, c, 0:MLA_IN])], hT_hi, hT_lo, h == 0, h == 1)
            pe.wait_ge(mod_ok, 3)
            gate_spread(1, 0, 4)
            pe.wait_ge(lat_ok, 1)
            for k in range(3):
                for c in range(TC):
                    ins = pe.transpose(ps[:, 2 + k // 2, (k % 2) * T + c * P:(k % 2) * T + (c + 1) * P],
                                       lat[:, c, k * P:(k + 1) * P], ident[:, :])
            ins.then_inc(lat_T, 1)
            pe.wait_ge(cTlo, 1)
            pe.wait_ge(gate_ok, 3)
            for u in range(2):
                product(M + 2 + u, 0, [(s * 384, 384, lambda c, s=s, u=u: ps[:, 4 * (1 - u) + 2 * c + s, 0:384])
                                       for s in range(2)], cT_hi, cT_lo, True, True)
            pe.wait_ge(ev_q, 8)
            n = no_of[M + 4]
            pe.wait_ge(freed, n + 1)
            for c in range(TC):
                for s in range(4):
                    ins = three(ps[:, 4 * c + s, :], cT_hi[:, 2, c * P:(c + 1) * P], cT_lo[:, 2, c * P:(c + 1) * P],
                                w_hi[(M + 4) % 2][:, s * 512:(s + 1) * 512], w_lo[(M + 4) % 2][:, s * 512:(s + 1) * 512],
                                True, True)
            ins.then_inc(used, 1)
            pe.wait_ge(ev_kv, 4)
            for h in range(MLA_H):
                for c in range(TC):
                    ins = pe.transpose(ps[:, 4 + h // 2, (h % 2) * T + c * P:(h % 2) * T + (c + 1) * P],
                                       qn[:, c, h * QW:h * QW + NOPE], ident[:, :])
            ins.then_inc(qT_mm, 1)
            pe.wait_ge(ev_kv, 8)
            for h in range(MLA_H):
                for c in range(TC):
                    ins = pe.transpose(ps[:, h // 2, (h % 2) * T + c * P:(h % 2) * T + (c + 1) * P],
                                       kvn[:, c, h * KVW:h * KVW + NOPE], ident[:, :])
            ins.then_inc(kT_mm, 1)
            pe.wait_ge(qT_ok, 1)
            pe.wait_ge(rope_ok, 1)
            for h in range(MLA_H):
                for c in range(TC):
                    ins = pe.transpose(ps[0:ROPE, 4 + h // 2, (h % 2) * T + c * P:(h % 2) * T + (c + 1) * P],
                                       qn[:, c, h * QW + NOPE:(h + 1) * QW], ident[:, :])
            ins.then_inc(rT_mm, 1)
            pe.wait_ge(kT_ok, 1)
            for c in range(TC):
                ins = pe.transpose(ps[0:ROPE, 0, c * P:(c + 1) * P], kr[:, c, :], ident[:, :])
            ins.then_inc(rT_mm, 1)
            pe.wait_ge(rT_d, 1)
            pe.wait_ge(rT_a, 1)
            for g in range(2):
                for h in range(4 * g, 4 * g + 4):
                    for q0, o, keys in ((0, ps[:, h, 0:P], P), (P, ps[:, h, P:3 * P], T)):
                        pe.matmul(o, qnT[:, h, q0:q0 + P], knT[:, h, 0:keys], start=True, stop=False)
                        ins = pe.matmul(o, qrT[:, h, q0:q0 + P], krT[:, 0:keys], start=False, stop=True)
                ins.then_inc(s_mm, 1)
            for g in range(2):
                pe.wait_ge(prob_ok, g + 1)
                for h in range(4):
                    for b in range(3):
                        ins = pe.transpose(ps[:, 4 * g + h, b * P:(b + 1) * P], prob[g][:, h, b, :], ident[:, :])
                ins.then_inc(pT_mm, 1)
            for g in range(2):
                pe.wait_ge(pT_ok, g + 1)
                weighted_values(g, prob, lambda c, h: kvn[:, c, h * KVW + NOPE:(h + 1) * KVW])
            pe.wait_ge(oT_lo, 4)
            M = first["mla_out"]
            for g in range(2):
                for h in range(2):
                    product(M + 2 * g + h, 4 * h, [(0, 512, bank(g, 2))], hT_hi, hT_lo, h == 0, h == 1, g + h == 2)
            mod_columns(3, 4)
            transpose_xhat(3)
            pe.wait_ge(hTlo, 16)
            pe.wait_ge(wr_cut, 2)
            for k in range(DC):
                for a in (wr_lo, wr_hi):
                    for b in (hT_lo, hT_hi):
                        ins = pe.matmul(ps[0:E, 3, 0:T], a[:, k, :], b[:, k, :],
                                        start=(k == 0 and a is wr_lo and b is hT_lo),
                                        stop=(k == DC - 1 and a is wr_hi and b is hT_hi))
            ins.then_inc(lgT_mm, 1)
            pe.wait_ge(lgT_ok, 1)
            for c in range(TC):
                ins = pe.transpose(ps[:, 3, c * E:(c + 1) * E], lgT[:, c * P:(c + 1) * P], ident[0:E, 0:E])
            ins.then_inc(lg_mm, 1)
            pe.wait_ge(mod_ok, 4)
            gate_spread(1, 1, 4)
            pe.wait_ge(member_ok, 1)
            for c in range(TC):
                o = ps[:, 3, 32 + c * E:32 + (c + 1) * E]
                if c:
                    pe.matmul(o, ones[:, :], member[:, 0, :], start=True, stop=False)
                pe.matmul(o, before[:, :], member[:, c, :], start=(c == 0), stop=True)
            for c in range(TC):
                ins = pe.matmul(ps[:, 3, 48:48 + E], ones[:, :], member[:, c, :], start=(c == 0), stop=(c == TC - 1))
            ins.then_inc(pos_mm, 1)

            def gather(visit_no):
                pe.wait_ge(e_pick, visit_no + 1)
                for b in range(2):
                    for a in range(4):
                        k = 4 * b + a
                        for c in range(TC):
                            for half in (xhat_hi, xhat_lo):
                                ins = pe.matmul(ps[:, b, a * P:(a + 1) * P], half[:, c, k * P:(k + 1) * P],
                                                pick[:, c, :], start=(c == 0 and half is xhat_hi),
                                                stop=(c == TC - 1 and half is xhat_lo))
                    ins.then_inc(e_gath, 1)

            def scatter(c, b0=6):
                for a in range(2):
                    for half in (ye_hi, ye_lo):
                        ins = pe.matmul(ps[:, b0 + a, :], spread[:, c * P:(c + 1) * P], half[:, a * 512:(a + 1) * 512],
                                        start=(half is ye_hi), stop=(half is ye_lo))
                ins.then_inc(e_sc, 1)

            pe.wait_ge(xs_lo, 1)
            gather(0)
            pe.wait_ge(visit_ok, 1)
            last = pe.value_load(n_end[0:1, 0:1], min_val=E, max_val=2 * E)
            with pe.Fori(0, last) as i:
                def expert_product(k, kc, lhs_hi, lhs_lo, k0, outs, total_k):
                    pe.wait_ge(freed, N0 + k + 1 + NK * i)
                    n_c = piece_elems(expert_piece(0, k)[1])
                    bh = m_hi[k % NB][:, 0:n_c].rearrange("p (k n) -> p k n", k=kc)
                    bl = m_lo[k % NB][:, 0:n_c].rearrange("p (k n) -> p k n", k=kc)
                    for c0, cn, out in outs:
                        for q in range(kc):
                            ins = three(out, lhs_hi[:, k0 + q, :], lhs_lo[:, k0 + q, :], bh[:, q, c0:c0 + cn],
                                        bl[:, q, c0:c0 + cn], k0 + q == 0, k0 + q == total_k - 1)
                    ins.then_inc(used, 1)

                def turn(j):
                    pe.wait_ge(e_hid, EG * i + j + 1)
                    if j >= 2:
                        pe.wait_ge(e_glo, EG * i + j - 1)
                    for a in range(gw[j] // P):
                        ins = pe.transpose(ps[:, 2 + j % 2, a * P:(a + 1) * P], ehid[j % 2][:, a * P:(a + 1) * P],
                                           ident[:, :])
                    ins.then_inc(e_hidT, 1)

                pe.wait_ge(e_xlo, 2 * i + 2)
                for j in range(EG):
                    if j >= 2:
                        pe.wait_ge(e_hid, EG * i + j - 1)
                    outs = [(0, 2 * gw[j], ps[:, j % 2, 0:2 * gw[j]])]
                    expert_product(2 * j, 4, xe_hi, xe_lo, 0, outs, DC)
                    if j >= 1:
                        turn(j - 1)
                    if j == 4:
                        pe.wait_ge(e_add, 2 * i + 2)
                        pe.wait_ge(e_pick, i + 1)
                        for c in range(TC):
                            ins = pe.matmul(ps[:, 6, c * P:(c + 1) * P], pick[:, c, :], ident_r[:, :], start=True,
                                            stop=True)
                        ins.then_inc(e_pT, 1)
                    expert_product(2 * j + 1, 4, xe_hi, xe_lo, 4, outs, DC)
                    if j == 1:
                        pe.wait_ge(e_ylo, i + 1)
                        scatter(0)
                    if j == 2:
                        pe.wait_ge(e_add, 2 * i + 1)
                        scatter(1)
                for d in range(EG):
                    pe.wait_ge(e_glo, EG * i + d + 1)
                    outs = [(a * 512, 512, ps[:, 4 + a, :]) for a in range(2)]
                    expert_product(2 * EG + d, dk[d], eT_hi, eT_lo, 2 * d, outs, EFC)
                    if d == 0:
                        turn(EG - 1)
                    if d == 1:
                        gather(i + 1)
            pe.wait_ge(e_ylo, last + 1)
            scatter(0)
            scatter(1, 4)


def kernel(**inputs):
    import numpy as np
    import concourse.bacc as bacc
    from concourse.bass_utils import run_bass_kernel_spmd as run

    nc = bacc.Bacc("TRN2", target_bir_lowering=False, num_devices=1)
    arrays, args = {}, []

    def given(name, a):
        a = np.ascontiguousarray(a)
        arrays["in_" + name] = a
        args.append(nc.dram_tensor("in_" + name, a.shape, mybir.dt.from_np(a.dtype), kind="ExternalInput").ap())

    for name in ("x", "c", "positions", "ada_w", "ada_b", "norm_g", "sb_w_in", "sb_w_out", "mla_w_in", "mla_g_q",
                 "mla_w_q_up", "mla_g_kv", "mla_w_kv_up", "mla_w_out", "ffn_w_gu", "ffn_w_down", "moe_w_router",
                 "moe_b_router", "moe_w_gu", "moe_w_down"):
        given(name, inputs[name])
    given("inv_freq", (np.float32(500000.0) ** (-np.arange(0, ROPE, 2, dtype=np.float32) / np.float32(ROPE)))
          .astype(np.float32)[None, :])
    out = nc.dram_tensor("out", (1, T, D), F32, kind="ExternalOutput").ap()
    trunk(nc, *args, out)
    return run(nc, [arrays], core_ids=[0]).results[0]["out"]
```
